# Optimizing a Trainium2 kernel written in Bass

```python
import jax
import jax.numpy as jnp
from jax import lax
import numpy as np

D_MODEL = 1024
BATCH = 1
SEQ = 256
DEPTH = 2

HEAD_DIM = 64
ROPE_THETA = 10000.0
Q_BLOCK = 128
LN_EPS = 1e-5
ALPHA = (2 * DEPTH) ** 0.25
BETA = (8 * DEPTH) ** -0.25

DIL_PATTERNS = ((128, 1), (512, 4), (2048, 16))
A_GROUPS = len(DIL_PATTERNS)
A_HEADS_PER_GROUP = 4
A_HEADS = A_GROUPS * A_HEADS_PER_GROUP
A_QKV = 3 * A_HEADS * HEAD_DIM
A_OUT = A_HEADS_PER_GROUP * HEAD_DIM

B_Q_HEADS = 8
B_KV_HEADS = 2
B_GROUP = B_Q_HEADS // B_KV_HEADS
B_Q = B_Q_HEADS * HEAD_DIM
B_KV = 3 * 2 * B_KV_HEADS * HEAD_DIM
B_GATE = 3 * B_Q_HEADS
CMP_STRIDE = 16
CMP_LEN = 2 * CMP_STRIDE
CMP_HIDDEN = 256
SLC_BLOCK = 64
SLC_TOPK = 8
WIN = 512

D_IN = A_QKV + B_Q + B_KV + B_GATE + 2 * D_MODEL

MEM_LEN = 256
X_HEADS = 4
X_DIM = X_HEADS * HEAD_DIM

D_FF = 2816
CONV_W = 3

kernel_name = 'hybrid_dilated_nsa_deepnorm_decoder'

def layer_norm(x, g, b):
    xf = x.astype(jnp.float32)
    mu = jnp.mean(xf, -1, keepdims=True)
    var = jnp.mean(jnp.square(xf - mu), -1, keepdims=True)
    y = (xf - mu) * lax.rsqrt(var + LN_EPS) * g.astype(jnp.float32) + b.astype(jnp.float32)
    return y.astype(x.dtype)

def rope(x, pos):
    half = HEAD_DIM // 2
    inv = ROPE_THETA ** (-jnp.arange(half, dtype=jnp.float32) / half)
    ang = pos.astype(jnp.float32)[:, None] * inv[None, :]
    cos = jnp.cos(ang)[None, :, None, :]
    sin = jnp.sin(ang)[None, :, None, :]
    xf = x.astype(jnp.float32)
    x1, x2 = xf[..., :half], xf[..., half:]
    return jnp.concatenate([x1 * cos - x2 * sin, x1 * sin + x2 * cos], -1).astype(x.dtype)

def masked_softmax(s, mask):
    s = jnp.where(mask, s.astype(jnp.float32), -jnp.inf)
    m = jnp.max(s, -1, keepdims=True)
    m = jnp.where(jnp.isfinite(m), m, 0.0)
    e = jnp.exp(s - m)
    l = jnp.maximum(jnp.sum(e, -1, keepdims=True), 1e-30)
    return e / l, (jnp.log(l) + m)[..., 0]

def dilated_window_attention(q, k, v, window, dilation):
    B, S, H, D = q.shape
    steps = window // dilation
    nq = Q_BLOCK // dilation
    nk = (window + Q_BLOCK) // dilation
    kp = jnp.pad(k, ((0, 0), (window, 0), (0, 0), (0, 0)))
    vp = jnp.pad(v, ((0, 0), (window, 0), (0, 0), (0, 0)))
    c = jnp.arange(nq)[:, None]
    a = jnp.arange(nk)[None, :]
    band = (c <= a) & (a <= steps + c)
    qb = q.reshape(B, S // Q_BLOCK, Q_BLOCK, H, D).swapaxes(0, 1)

    def block(args):
        i, qi = args
        s0 = i * Q_BLOCK
        kb = lax.dynamic_slice_in_dim(kp, s0, window + Q_BLOCK, axis=1).reshape(B, nk, dilation, H, D)
        vb = lax.dynamic_slice_in_dim(vp, s0, window + Q_BLOCK, axis=1).reshape(B, nk, dilation, H, D)
        qr = qi.reshape(B, nq, dilation, H, D)
        valid = band & (s0 - window + a * dilation >= 0)
        s = jnp.einsum('bcrhd,barhd->bhrca', qr, kb) * D ** -0.5
        p, lse = masked_softmax(s, valid)
        o = jnp.einsum('bhrca,barhd->bcrhd', p.astype(v.dtype), vb)
        return o.reshape(B, Q_BLOCK, H, D), lse.transpose(0, 3, 2, 1).reshape(B, Q_BLOCK, H)

    o, lse = lax.map(block, (jnp.arange(S // Q_BLOCK), qb))
    return o.swapaxes(0, 1).reshape(B, S, H, D), lse.swapaxes(0, 1).reshape(B, S, H)

def compress_blocks(x, pos_emb, w1, b1, w2):
    B, S, H, D = x.shape
    ch = x.reshape(B, S // CMP_STRIDE, CMP_STRIDE, H, D)
    blk = jnp.concatenate([ch[:, :-1], ch[:, 1:]], axis=2) + pos_emb[None, None, :, None, :]
    nc = blk.shape[1]
    flat = blk.transpose(0, 1, 3, 2, 4).reshape(B, nc, H, CMP_LEN * D)
    return jax.nn.gelu(flat @ w1 + b1) @ w2

def nsa_attention(q, kc, vc, ks, vs, kw, vw):
    B, S, Hq, D = q.shape
    Hkv = B_KV_HEADS
    nc = kc.shape[1]
    ns = S // SLC_BLOCK
    n_sel = min(SLC_TOPK, ns)
    scale = D ** -0.5
    c_start = CMP_STRIDE * jnp.arange(nc)
    c_end = c_start + CMP_LEN - 1
    s_start = SLC_BLOCK * jnp.arange(ns)
    overlap = jnp.clip(jnp.minimum(c_start[:, None] + CMP_LEN, s_start[None, :] + SLC_BLOCK)
                       - jnp.maximum(c_start[:, None], s_start[None, :]), 0).astype(jnp.float32) / CMP_LEN
    ks_blk = ks.reshape(B, ns, SLC_BLOCK, Hkv, D).transpose(0, 3, 1, 2, 4)
    vs_blk = vs.reshape(B, ns, SLC_BLOCK, Hkv, D).transpose(0, 3, 1, 2, 4)
    kw_p = jnp.pad(kw, ((0, 0), (WIN, 0), (0, 0), (0, 0)))
    vw_p = jnp.pad(vw, ((0, 0), (WIN, 0), (0, 0), (0, 0)))
    b_ix = jnp.arange(B)[:, None, None]
    h_ix = jnp.arange(Hkv)[None, :, None]
    blk_ids = jnp.arange(ns)
    qb = q.reshape(B, S // Q_BLOCK, Q_BLOCK, Hkv, B_GROUP, D).swapaxes(0, 1)

    def block(args):
        i, qi = args
        s0 = i * Q_BLOCK
        t = s0 + jnp.arange(Q_BLOCK)
        s = jnp.einsum('bqkgd,bnkd->bkgqn', qi, kc) * scale
        p_c, _ = masked_softmax(s, c_end[None, :] <= t[:, None])
        o_c = jnp.einsum('bkgqn,bnkd->bqkgd', p_c.astype(vc.dtype), vc)
        imp = jnp.einsum('bkgqn,nm->bkqm', p_c, overlap)
        cur = t // SLC_BLOCK
        forced = (blk_ids[None, :] == 0) | (blk_ids[None, :] == cur[:, None]) | (blk_ids[None, :] == cur[:, None] - 1)
        future = blk_ids[None, :] * SLC_BLOCK > t[:, None]
        imp = jnp.where(future, -jnp.inf, jnp.where(forced, jnp.inf, imp))
        _, idx = lax.top_k(imp, n_sel)
        idx_f = idx.reshape(B, Hkv, Q_BLOCK * n_sel)
        kg = ks_blk[b_ix, h_ix, idx_f].reshape(B, Hkv, Q_BLOCK, n_sel * SLC_BLOCK, D)
        vg = vs_blk[b_ix, h_ix, idx_f].reshape(B, Hkv, Q_BLOCK, n_sel * SLC_BLOCK, D)
        tok = (idx[..., None] * SLC_BLOCK + jnp.arange(SLC_BLOCK)).reshape(B, Hkv, Q_BLOCK, n_sel * SLC_BLOCK)
        s = jnp.einsum('bqkgd,bkqtd->bkgqt', qi, kg) * scale
        p_s, _ = masked_softmax(s, (tok <= t[None, None, :, None])[:, :, None])
        o_s = jnp.einsum('bkgqt,bkqtd->bqkgd', p_s.astype(vg.dtype), vg)
        kwb = lax.dynamic_slice_in_dim(kw_p, s0, WIN + Q_BLOCK, axis=1)
        vwb = lax.dynamic_slice_in_dim(vw_p, s0, WIN + Q_BLOCK, axis=1)
        kpos = s0 - WIN + jnp.arange(WIN + Q_BLOCK)
        dist = t[:, None] - kpos[None, :]
        wmask = (dist >= 0) & (dist < WIN) & (kpos[None, :] >= 0)
        s = jnp.einsum('bqkgd,btkd->bkgqt', qi, kwb) * scale
        p_w, _ = masked_softmax(s, wmask)
        o_w = jnp.einsum('bkgqt,btkd->bqkgd', p_w.astype(vw.dtype), vwb)
        return jnp.stack([o_c, o_s, o_w], axis=-2)

    o = lax.map(block, (jnp.arange(S // Q_BLOCK), qb))
    return o.swapaxes(0, 1).reshape(B, S, Hq, 3, D)

def hybrid_mixer(h, pos, w_in, cmp_pos, cmp_w1, cmp_b1, cmp_w2, w_branch_a, w_branch_b, w_mix_out):
    B, S, _ = h.shape
    z = h @ w_in
    o1 = A_QKV
    o2 = o1 + B_Q
    o3 = o2 + B_KV
    o4 = o3 + B_GATE
    o5 = o4 + D_MODEL
    z_a, z_bq, z_bkv, z_bg, z_ga, z_gb = jnp.split(z, [o1, o2, o3, o4, o5], axis=-1)

    qkv_a = z_a.reshape(B, S, 3, A_GROUPS, A_HEADS_PER_GROUP, HEAD_DIM)
    outs, lses = [], []
    for g, (window, dilation) in enumerate(DIL_PATTERNS):
        o_g, l_g = dilated_window_attention(rope(qkv_a[:, :, 0, g], pos), rope(qkv_a[:, :, 1, g], pos),
                                            qkv_a[:, :, 2, g], window, dilation)
        outs.append(o_g)
        lses.append(l_g)
    wts = jax.nn.softmax(jnp.stack(lses), axis=0)
    y_a = jnp.sum(wts[..., None].astype(h.dtype) * jnp.stack(outs), axis=0).reshape(B, S, A_OUT)

    q_b = rope(z_bq.reshape(B, S, B_Q_HEADS, HEAD_DIM), pos)
    kv = z_bkv.reshape(B, S, 3, 2, B_KV_HEADS, HEAD_DIM)
    kc = compress_blocks(kv[:, :, 0, 0], cmp_pos[0], cmp_w1[0], cmp_b1[0], cmp_w2[0])
    vc = compress_blocks(kv[:, :, 0, 1], cmp_pos[1], cmp_w1[1], cmp_b1[1], cmp_w2[1])
    kc = rope(kc, CMP_STRIDE * jnp.arange(kc.shape[1]) + CMP_LEN - 1)
    o_b = nsa_attention(q_b, kc, vc, rope(kv[:, :, 1, 0], pos), kv[:, :, 1, 1],
                        rope(kv[:, :, 2, 0], pos), kv[:, :, 2, 1])
    g_b = jax.nn.sigmoid(z_bg.reshape(B, S, B_Q_HEADS, 3))
    y_b = jnp.sum(g_b[..., None] * o_b, axis=-2).reshape(B, S, B_Q)

    merged = jax.nn.sigmoid(z_ga) * (y_a @ w_branch_a) + jax.nn.sigmoid(z_gb) * (y_b @ w_branch_b)
    return merged @ w_mix_out

def memory_cross_attention(h, mem, w_xq, w_xkv, w_xo):
    B, S, _ = h.shape
    M = mem.shape[1]
    q = (h @ w_xq).reshape(B, S, X_HEADS, HEAD_DIM)
    kv = (mem @ w_xkv).reshape(B, M, 2, X_HEADS, HEAD_DIM)
    s = jnp.einsum('bshd,bmhd->bhsm', q, kv[:, :, 0]).astype(jnp.float32) * HEAD_DIM ** -0.5
    p = jax.nn.softmax(s, axis=-1).astype(h.dtype)
    o = jnp.einsum('bhsm,bmhd->bshd', p, kv[:, :, 1]).reshape(B, S, X_DIM)
    return o @ w_xo

def causal_dwconv(u, w, b):
    C = u.shape[-1]
    y = lax.conv_general_dilated(u, w[:, None, :].astype(u.dtype), window_strides=(1,),
                                 padding=[(CONV_W - 1, 0)], dimension_numbers=('NWC', 'WIO', 'NWC'),
                                 feature_group_count=C)
    return y + b

def conv_ffn(h, w_up, conv_w, conv_b, w_down):
    u = causal_dwconv(h @ w_up, conv_w, conv_b)
    a, g = jnp.split(u, 2, axis=-1)
    return (jax.nn.gelu(a) * g) @ w_down

def _normal(key, shape, scale):
    return jax.random.normal(key, shape, jnp.float32) * scale

def setup_inputs(seed: int = 0) -> dict:
    key = jax.random.key(seed)
    ks = jax.random.split(key, 23)
    D = D_MODEL
    L = DEPTH
    return {
        'x': _normal(ks[0], (BATCH, SEQ, D), 1.0),
        'mem': _normal(ks[1], (BATCH, MEM_LEN, D), 1.0),
        'w_in': _normal(ks[2], (L, D, D_IN), D ** -0.5),
        'cmp_pos': _normal(ks[3], (L, 2, CMP_LEN, HEAD_DIM), 0.02),
        'cmp_w1': _normal(ks[4], (L, 2, CMP_LEN * HEAD_DIM, CMP_HIDDEN), (CMP_LEN * HEAD_DIM) ** -0.5),
        'cmp_b1': _normal(ks[5], (L, 2, CMP_HIDDEN), 0.01),
        'cmp_w2': _normal(ks[6], (L, 2, CMP_HIDDEN, HEAD_DIM), CMP_HIDDEN ** -0.5),
        'w_branch_a': _normal(ks[7], (L, A_OUT, D), A_OUT ** -0.5),
        'w_branch_b': _normal(ks[8], (L, B_Q, D), B_Q ** -0.5),
        'w_mix_out': _normal(ks[9], (L, D, D), BETA * D ** -0.5),
        'ln1_g': 1.0 + _normal(ks[10], (L, D), 0.02),
        'ln1_b': _normal(ks[11], (L, D), 0.02),
        'w_xq': _normal(ks[12], (L, D, X_DIM), D ** -0.5),
        'w_xkv': _normal(ks[13], (L, D, 2 * X_DIM), D ** -0.5),
        'w_xo': _normal(ks[14], (L, X_DIM, D), BETA * X_DIM ** -0.5),
        'ln2_g': 1.0 + _normal(ks[15], (L, D), 0.02),
        'ln2_b': _normal(ks[16], (L, D), 0.02),
        'w_up': _normal(ks[17], (L, D, 2 * D_FF), D ** -0.5),
        'conv_w': _normal(ks[18], (L, CONV_W, 2 * D_FF), CONV_W ** -0.5),
        'conv_b': _normal(ks[19], (L, 2 * D_FF), 0.01),
        'w_down': _normal(ks[20], (L, D_FF, D), BETA * D_FF ** -0.5),
        'ln3_g': 1.0 + _normal(ks[21], (L, D), 0.02),
        'ln3_b': _normal(ks[22], (L, D), 0.02),
    }

def reference(x, mem, w_in, cmp_pos, cmp_w1, cmp_b1, cmp_w2, w_branch_a, w_branch_b, w_mix_out,
              ln1_g, ln1_b, w_xq, w_xkv, w_xo, ln2_g, ln2_b, w_up, conv_w, conv_b, w_down, ln3_g, ln3_b):
    pos = jnp.arange(x.shape[1])
    h = x
    for l in range(DEPTH):
        mix = hybrid_mixer(h, pos, w_in[l], cmp_pos[l], cmp_w1[l], cmp_b1[l], cmp_w2[l],
                           w_branch_a[l], w_branch_b[l], w_mix_out[l])
        h = layer_norm(ALPHA * h + mix, ln1_g[l], ln1_b[l])
        h = layer_norm(ALPHA * h + memory_cross_attention(h, mem, w_xq[l], w_xkv[l], w_xo[l]), ln2_g[l], ln2_b[l])
        h = layer_norm(ALPHA * h + conv_ffn(h, w_up[l], conv_w[l], conv_b[l], w_down[l]), ln3_g[l], ln3_b[l])
    return h


_drawn_inputs = setup_inputs


def setup_inputs(seed=0):
    import zlib

    import numpy as np

    out = dict(_drawn_inputs(seed))
    spreads = {}
    factors = {'cmp_pos': 34.401, 'cmp_b1': 64.0, 'conv_b': 8.0}
    for name, (base, spread) in spreads.items():
        noise = np.random.default_rng([zlib.crc32(name.encode()), seed]).standard_normal(out[name].shape)
        drawn = base * np.exp(spread * noise) if base else spread * noise
        out[name] = jnp.asarray(drawn.astype(out[name].dtype))
    for name, factor in factors.items():
        out[name] = (out[name] * factor).astype(out[name].dtype)
    return out
```

```python
from contextlib import ExitStack

import numpy as np

import concourse.bass as bass
from concourse import mybir

F32 = mybir.dt.float32
F32R = mybir.dt.float32r
BF16 = mybir.dt.bfloat16
I32 = mybir.dt.int32
ACT = mybir.ActivationFunctionType
ALU = mybir.AluOpType
AX = mybir.AxisListType

P = 128
D = 1024
S = 256
TT = S // P
DEPTH = 2
HD = 64
KT = D // P
A_GROUPS, A_HPG = 3, 4
DIL = ((128, 1), (512, 4), (2048, 16))
BQ_HEADS, BKV_HEADS = 8, 2
CMP_STRIDE, CMP_LEN, CMP_HID = 16, 32, 256
NBLK = S // CMP_STRIDE - 1
FF = 2816
X_HEADS = 4
ALPHA = (2 * DEPTH) ** 0.25
LN_EPS = 1e-5
SCALE = HD ** -0.5
NEG = -1e30
FLOOR = -1e29
THETA = 10000.0

COL_BG = 3 * A_GROUPS * A_HPG * HD + BQ_HEADS * HD + 6 * BKV_HEADS * HD
N_BG = 3 * BQ_HEADS
COL_GATE = COL_BG + N_BG

UNIT = 2048
RAW, SPLIT = 3, 4

Z_PLACES = (4, 5, 0, 1, "cmp", 2, 3, 6)
FF_IT = FF // 256


def plan_units():
    u = []
    for c in Z_PLACES:
        if c == "cmp":
            u += [("cmp", kv, half) for kv in (0, 1) for half in (0, 1)]
        else:
            u += [("z", c, half) for half in (0, 1)]
    u += [("bg",)]
    u += [("xkv", 0), ("xkv", 1)]
    u += [("gate", c, half) for c in range(4) for half in (0, 1)]
    u += [("wa",), ("wb", 0), ("wb", 1)]
    u += [("mix", n, half) for n in (0, 1) for half in (0, 1)]
    u += [("xq",), ("xo",)]
    for it in range(FF_IT):
        u += [("ua", it), ("ug", it)]
        if it:
            u += [("down", it - 1)]
    u += [("down", FF_IT - 1)]
    return u


UNITS = plan_units()
NU = len(UNITS)
UNIT_AT = {name: i for i, name in enumerate(UNITS)}

ITEMS = [("A", h, tt) for h in range(A_HPG) for tt in range(TT)]
ITEMS += [("C", None, tt) for tt in range(TT)]
ITEMS += [("B", (2 * p, 2 * p + 1), 0) for p in range(BQ_HEADS // 2)]
ITEMS += [("B", (h,), 1) for h in range(BQ_HEADS)]
NI = len(ITEMS)
FIRST_GATE = 4
assert FIRST_GATE + 16 <= NI

Z_GROUPS = {1: ["cmp", "bq"], 2: [0], 3: [1], 4: ["hid"], 5: [2, "cmp2"], 6: ["kct"], 7: ["sw"]}
TWO = ("cmp", "bq", "hid", "sw", 0, 1, 2)
Z_T = sum(2 if kind in TWO else 1 for v in Z_GROUPS.values() for kind in v)


def groups_until(kind):
    n = 0
    for place in sorted(Z_GROUPS):
        for other in Z_GROUPS[place]:
            n += 2 if other in TWO else 1
            if other == kind:
                return n


STAGING_FREE = {2: groups_until("bq"), 3: groups_until("bq"), 5: groups_until(1), 7: groups_until(2)}
ROPES_BEFORE = {"bq": 2, 0: 3, 1: 4, 2: 5, "sw": 6}
BG_EVAC = len(Z_PLACES) + 1

PER = dict(unit=NU, z_evac=BG_EVAC + 4, zt=Z_T, roped=6, item=NI, yt=3, ht=16, ln=6, conv=2 * FF_IT, ffn=FF_IT, x=4)
HT0 = 8

F_ID, F_COS, F_SIN, F_BD, F_KC, F_KS, F_END = 0, 128, 256, 384, 392, 456, 520
B_ID, B_A0, B_A1, B_B0, B_B1, B_C, B_END = 0, 128, 512, 1280, 1408, 1664, 1696
T_CONV, T_CB, T_POS, T_B1, T_END = 0, 132, 176, 208, 212


def shape_constants():
    half = HD // 2
    inv = (np.float32(THETA) ** (-np.arange(half, dtype=np.float32) / np.float32(half))).astype(np.float32)

    def rope_rows(pos):
        ang = pos.astype(np.float32)[:, None] * inv[None, :]
        c, s = np.cos(ang).astype(np.float32), np.sin(ang).astype(np.float32)
        return np.concatenate([c, c], 1), np.concatenate([-s, s], 1)

    f = np.zeros((P, F_END), np.float32)
    f[:, F_ID:F_ID + P] = np.eye(P)
    for tt in range(TT):
        c, s = rope_rows(np.arange(tt * P, (tt + 1) * P))
        f[:, F_COS + HD * tt:F_COS + HD * (tt + 1)] = c
        f[:, F_SIN + HD * tt:F_SIN + HD * (tt + 1)] = s
    f[np.arange(P), F_BD + np.arange(P) // 16] = 1.0
    c, s = rope_rows(CMP_STRIDE * np.arange(NBLK) + CMP_LEN - 1)
    f[:NBLK, F_KC:F_KC + HD] = c
    f[:NBLK, F_KS:F_KS + HD] = s
    b = np.zeros((P, B_END), np.float32)
    b[:, B_ID:B_ID + P] = np.eye(P)
    for tt, at_a, at_b in ((0, B_A0, B_B0), (1, B_A1, B_B1)):
        w = P * (tt + 1)
        dist = (tt * P + np.arange(P))[:, None] - np.arange(w)[None, :]
        for g, (window, dil) in enumerate(DIL):
            ok = (dist >= 0) & (dist <= window) & (dist % dil == 0)
            b[:, at_a + g * w:at_a + (g + 1) * w] = np.where(ok, 0.0, NEG)
        b[:, at_b:at_b + w] = np.where(dist >= 0, 0.0, NEG)
        ends = CMP_STRIDE * np.arange(16) + CMP_LEN - 1
        ok = (ends[None, :] <= (tt * P + np.arange(P))[:, None]) & (np.arange(16) < NBLK)[None, :]
        b[:, B_C + 16 * tt:B_C + 16 * (tt + 1)] = np.where(ok, 0.0, NEG)
    return f, b


def hybrid_decoder_kernel(nc, w, const_f, const_b, out):
    with ExitStack() as ctx:
        def sb(name, shape, dt=F32):
            return ctx.enter_context(nc.sbuf_tensor(name, shape, dt))

        def sem(name):
            return ctx.enter_context(nc.semaphore(name))

        raw = sb("raw", [P, RAW, UNIT])
        w_hi = sb("w_hi", [P, SPLIT, UNIT], F32R)
        w_lo = sb("w_lo", [P, SPLIT, UNIT], F32R)
        h = sb("h", [P, TT, D])
        hT_hi = sb("hT_hi", [P, KT, S], F32R)
        hT_lo = sb("hT_lo", [P, KT, S], F32R)
        memT_hi = sb("memT_hi", [P, KT, S], F32R)
        memT_lo = sb("memT_lo", [P, KT, S], F32R)
        cf = sb("cf", [P, F_END])
        cb = sb("cb", [P, B_END], BF16)
        ptab = sb("ptab", [P, T_END])
        w2 = sb("w2", [P, 2, 2, HD])
        hid = sb("hid", [P, 2, 2, BQ_HEADS, 16])
        kcT = sb("kcT", [P, 16])
        cs = sb("cs", [P, BQ_HEADS, 16])
        bgt = sb("bgt", [P, TT, N_BG])
        stat = sb("stat", [P, 4, 64])
        coef = sb("coef", [P, 64])
        xstat = sb("xstat", [P, 4, 8])
        lnst = sb("lnst", [P, TT, 2, 6])
        lnmv = sb("lnmv", [P, TT, 2])
        lnv = sb("lnv", [P, TT, 8])

        def arena(name, size):
            base = nc.sbuf_base
            sb(name, [P, size // 4])

            def at(label, shape, offset, dt=F32):
                return nc.alloc_sbuf_tensor_at(label, shape, dt, offset=base + offset)
            return at

        arena_0 = arena("arena_0", 8192)
        gb = arena_0("gb", [P, 2, D], 0)
        prob = arena_0("prob", [P, 2, 768], 0)
        hidn = arena_0("hidn", [2 * NBLK, 2, CMP_HID], 6144)

        arena_1 = arena("arena_1", 16384)
        staging = arena_1("staging", [P, 2, TT, 512], 0)
        const_staged = arena_1("const_staged", [P, B_END], 0)
        rope_a = arena_1("rope_a", [P, TT, 512], 8192)
        rope_b = arena_1("rope_b", [P, TT, 512], 12288)
        xv = arena_1("xv", [P, 2, S], 0)
        probT = arena_1("probT", [P, 2, 768], 3072)
        y = arena_1("y", [P, TT, 768], 9216)
        conv_y = arena_1("conv_y", [P, 2, 2, 2, S], 0)
        gelu_a = arena_1("gelu_a", [P, 2, S], 8192)
        hidf = arena_1("hidf", [P, 2, S], 10240)

        arena_2 = arena("arena_2", 16384)
        gates = arena_2("gates", [P, 4, TT, 512], 0)
        cmpx = arena_2("cmpx", [P, TT, 4, 2, HD], 0)
        xT2 = arena_2("xT2", [P, 4, S], 4096)
        blk_hi = arena_2("blk_hi", [P, 2, 16, 2 * NBLK], 8192, F32R)
        blk_lo = arena_2("blk_lo", [P, 2, 16, 2 * NBLK], 12288, F32R)
        vcbd = arena_2("vcbd", [P, BQ_HEADS, HD], 8192)
        kcn = arena_2("kcn", [16, 4, P], 10240)
        vcn = arena_2("vcn", [P, HD], 12288)
        xqT = arena_2("xqT", [P, 2, S], 0)
        xprob = arena_2("xprob", [P, 2, 512], 2048)
        xo_n = arena_2("xo_n", [P, TT, S], 6144)
        xoT_hi = arena_2("xoT_hi", [P, 2, S], 8192, F32R)
        xoT_lo = arena_2("xoT_lo", [P, 2, S], 10240, F32R)
        hid_hi = arena_2("hid_hi", [P, 2, 2, S], 0, F32R)
        hid_lo = arena_2("hid_lo", [P, 2, 2, S], 4096, F32R)

        arena_3 = arena("arena_3", 12288 + 4096)
        qkT = arena_3("qkT", [P, 12, S], 0)
        blkf = arena_3("blkf", [P, 2, 16, 2 * NBLK], 8192)
        yT_hi = arena_3("yT_hi", [P, 6, S], 0, F32R)
        yT_lo = arena_3("yT_lo", [P, 6, S], 6144, F32R)
        bqT = arena_3("bqT", [P, 4, S], 12288)
        prm_c = arena_3("prm_c", [44, 4, P], 12288)
        prm_p = arena_3("prm_p", [16, 2, P], 12288 + 2048)
        prm_b = arena_3("prm_b", [4, P], 12288 + 3072)

        va = sb("va", [P, TT, 768])
        bv = sb("bv", [P, TT, 2, P])
        swT = sb("swT", [P, 2, S])
        xkT = sb("xkT", [P, 2, S])

        ps = ctx.enter_context(nc.psum_tensor("ps", [P, 8, 512], F32))
        flat = ps[:, :, :].rearrange("p b n -> p (b n)")

        ident = cf[:, F_ID:F_ID + P]
        identb = cb[:, B_ID:B_ID + P]

        const_loaded = sem("const_loaded")
        cb_ready = sem("cb_ready")
        act_in_loaded = sem("act_in_loaded")
        raw_loaded = [sem(f"raw_loaded{i}") for i in range(RAW)]
        hi_split = sem("hi_split")
        lo_split = sem("lo_split")
        unit_used = sem("unit_used")
        gb_loaded = sem("gb_loaded")
        prm_loaded = sem("prm_loaded")
        prm_turned = sem("prm_turned")
        ptab_ready = sem("ptab_ready")
        z_evac = sem("z_evac")
        zt_turned = sem("zt_turned")
        zt_evac = sem("zt_evac")
        roped = sem("roped")
        hid_zeroed = sem("hid_zeroed")
        blkf_ready = sem("blkf_ready")
        blk_hi_ready = sem("blk_hi_ready")
        blk_lo_ready = sem("blk_lo_ready")
        cmp_vec = sem("cmp_vec")
        bg_ready = sem("bg_ready")
        scores_done = sem("scores_done")
        shift_ready = sem("shift_ready")
        exp_done = sem("exp_done")
        probT_done = sem("probT_done")
        probT_evac = sem("probT_evac")
        pv_done = sem("pv_done")
        o_evac = sem("o_evac")
        yT_done = sem("yT_done")
        yT_hi_ready = sem("yT_hi_ready")
        yT_lo_ready = sem("yT_lo_ready")
        a_gated = sem("a_gated")
        merged = sem("merged")
        xkv_ready = sem("xkv_ready")
        hT_turned = sem("hT_turned")
        hT_hi_ready = sem("hT_hi_ready")
        hT_lo_ready = sem("hT_lo_ready")
        res_done = sem("res_done")
        ln_done = sem("ln_done")
        xq_ready = sem("xq_ready")
        x_scores = sem("x_scores")
        x_shift = sem("x_shift")
        x_exp = sem("x_exp")
        x_turned = sem("x_turned")
        x_probT = sem("x_probT")
        x_pv = sem("x_pv")
        x_evac = sem("x_evac")
        xoT_done = sem("xoT_done")
        xoT_hi_ready = sem("xoT_hi_ready")
        xoT_lo_ready = sem("xoT_lo_ready")
        conv_first = sem("conv_first")
        conv_done = sem("conv_done")
        gelu_done = sem("gelu_done")
        hidf_ready = sem("hidf_ready")
        hid_hi_ready = sem("hid_hi_ready")
        hid_lo_ready = sem("hid_lo_ready")
        out_stored = sem("out_stored")
        dve_step = sem("dve_step")

        def unit_view(t, slot, name):
            kind = name[0]
            if kind == "bg":
                return t[:, slot, 0:KT * N_BG].rearrange("p (k n) -> p k n", k=KT)
            k = {"z": 4, "gate": 4, "wb": 4, "xkv": 4, "mix": 4, "wa": 2, "xo": 2, "down": 2}.get(kind, 8)
            return t[:, slot, :].rearrange("p (k n) -> p k n", k=k)

        def unit_source(layer, name):
            kind = name[0]
            if kind in ("z", "gate"):
                col = 512 * name[1] + (COL_GATE if kind == "gate" else 0)
                src = w["w_in"][layer, 512 * name[2]:512 * (name[2] + 1), col:col + 512]
            elif kind == "bg":
                src = w["w_in"][layer, :, COL_BG:COL_BG + N_BG]
            elif kind == "cmp":
                src = w["cmp_w1"][layer, name[1], 1024 * name[2]:1024 * (name[2] + 1), :]
            elif kind == "wa":
                src = w["w_branch_a"][layer, :, :]
            elif kind == "wb":
                src = w["w_branch_b"][layer, :, 512 * name[1]:512 * (name[1] + 1)]
            elif kind == "xkv":
                src = w["w_xkv"][layer, 512 * name[1]:512 * (name[1] + 1), :]
            elif kind == "mix":
                src = w["w_mix_out"][layer, 512 * name[2]:512 * (name[2] + 1), 512 * name[1]:512 * (name[1] + 1)]
            elif kind == "xq":
                src = w["w_xq"][layer, :, :]
            elif kind == "xo":
                src = w["w_xo"][layer, :, :]
            elif kind == "ua":
                src = w["w_up"][layer, :, 256 * name[1]:256 * (name[1] + 1)]
            elif kind == "ug":
                src = w["w_up"][layer, :, FF + 256 * name[1]:FF + 256 * (name[1] + 1)]
            else:
                src = w["w_down"][layer, 256 * name[1]:256 * (name[1] + 1), :]
            return src.rearrange("(k p) n -> p k n", p=P)

        def item_width(tt):
            return P * (tt + 1)

        def item_rows(item):
            kind, heads, tt = item
            return 1 if kind == "A" else 2 * len(heads) if kind == "B" else BQ_HEADS

        def item_blocks(item):
            kind, heads, tt = item
            return 1 if kind == "C" else 3 * (tt + 1) if kind == "A" else 4

        def stat_column(i):
            return sum(item_rows(x) for x in ITEMS[:i])

        def score_at(i):
            return 1024 * (1 + i % 2)

        TURNED, OUT = 6 * 512, 7 * 512 + 256

        block = ctx.enter_context(nc.Block())

        @block.sync
        def _(sp):
            sp.dma_start(cf[:, :], const_f).then_inc(const_loaded, 16)
            sp.dma_start(h[:, :, :], w["mem"][0].rearrange("(t p) d -> p t d", p=P)).then_inc(act_in_loaded, 16)
            sp.dma_start(const_staged[:, :], const_b).then_inc(const_loaded, 16)
            for layer in range(DEPTH):
                for u, name in enumerate(UNITS):
                    n = layer * NU + u
                    if n >= RAW:
                        sp.wait_ge(lo_split, n - RAW + 1)
                    if n == 3:
                        sp.wait_ge(hT_turned, 4)
                        sp.dma_start(h[:, :, :], w["x"][0].rearrange("(t p) d -> p t d", p=P)).then_inc(act_in_loaded, 16)
                    sp.dma_start(unit_view(raw, n % RAW, name), unit_source(layer, name)).then_inc(raw_loaded[n % RAW], 16)
            for tt in range(TT):
                sp.wait_ge(ln_done, DEPTH * PER["ln"] - TT + tt + 1)
                sp.dma_start(out[0, tt * P:(tt + 1) * P, :], h[:, tt, :]).then_inc(out_stored, 16)
            sp.wait_ge(out_stored, 16 * TT)

        @block.gpsimd
        def _(pool):
            pool.memset(hid[:, :, :, :, :], 0.0).then_inc(hid_zeroed, 1)
            for layer in range(DEPTH):
                if layer:
                    pool.wait_ge(x_evac, layer * PER["x"])
                t = w["conv_w"][layer].rearrange("i (t p) -> t i p", p=P)
                pool.dma_start(prm_c[:, 0:3, :], t).then_inc(prm_loaded, 16)
                t = w["conv_b"][layer].rearrange("(t p) -> t p", p=P)
                pool.dma_start(prm_c[:, 3, :], t).then_inc(prm_loaded, 16)
                t = w["cmp_pos"][layer].rearrange("v (j a) d -> j v (a d)", a=2)
                pool.dma_start(prm_p[:, :, :], t).then_inc(prm_loaded, 16)
                t = w["cmp_b1"][layer].rearrange("v (m p) -> (v m) p", p=P)
                pool.dma_start(prm_b[:, :], t).then_inc(prm_loaded, 16)
                t = w["cmp_w2"][layer].rearrange("v (m p) d -> p v m d", p=P)
                pool.dma_start(w2[:, :, :, :], t).then_inc(prm_loaded, 16)
                for k, (g, b) in enumerate((("ln1_g", "ln1_b"), ("ln2_g", "ln2_b"), ("ln3_g", "ln3_b"))):
                    if k == 0:
                        pool.wait_ge(probT_done, NI * (layer + 1))
                    else:
                        pool.wait_ge(ln_done, layer * PER["ln"] + 2 * k)
                    pool.dma_start(gb[:, 0, :], w[g][layer:layer + 1, :].partition_broadcast(P)).then_inc(gb_loaded, 16)
                    pool.dma_start(gb[:, 1, :], w[b][layer:layer + 1, :].partition_broadcast(P)).then_inc(gb_loaded, 16)

        @block.scalar
        def _(act):
            done = [0]

            def split_through(n):
                while done[0] <= n and done[0] < DEPTH * NU:
                    k = done[0]
                    act.wait_ge(raw_loaded[k % RAW], 16 * (k // RAW + 1))
                    if k >= SPLIT:
                        act.wait_ge(unit_used, k - SPLIT + 1)
                    size = KT * N_BG if UNITS[k % NU] == ("bg",) else UNIT
                    act.copy(w_hi[:, k % SPLIT, 0:size], raw[:, k % RAW, 0:size]).then_inc(hi_split, 1)
                    done[0] += 1

            def ahead(layer, name):
                split_through(layer * NU + UNIT_AT[name] + SPLIT - 1)

            def used(layer, name):
                act.wait_ge(unit_used, layer * NU + UNIT_AT[name] + 1)

            def hT_high(group, bank, dst, tile0, tt, scale=1.0):
                act.wait_ge(hT_turned, group + 1)
                act.activation(dst[:, tile0:tile0 + 4, tt * P:(tt + 1) * P],
                               ps[:, bank, :].rearrange("p (t n) -> p t n", n=P),
                               ACT.Identity, scale=scale).then_inc(hT_hi_ready, 1)

            def layer_norm_high(layer, k):
                for tt in range(TT):
                    for half in (0, 1):
                        hT_high(HT0 + layer * PER["ht"] + 4 * (k + 1) + 2 * tt + half, 4 + 2 * tt + half, hT_hi, 4 * half, tt)

            for g in range(4):
                hT_high(g, g, memT_hi, 4 * (g % 2), g // 2)
            act.wait_ge(const_loaded, 32)
            act.copy(cb[:, :], const_staged[:, :]).then_inc(cb_ready, 1)
            split_through(2)
            for g in range(4):
                hT_high(4 + g, 4 + g, hT_hi, 4 * (g % 2), g // 2)

            for layer in range(DEPTH):
                base = layer * PER["z_evac"]
                zt = layer * PER["zt"]
                act.wait_ge(prm_turned, layer + 1)
                act.copy(ptab[:, :], ps[:, 4, 0:T_END]).then_inc(ptab_ready, 1)

                group = [0]

                def turn_evac(place):
                    for kind in Z_GROUPS.get(place, ()):
                        for tt in range(TT if kind in TWO else 1):
                            act.wait_ge(zt_turned, zt + group[0] + 1)
                            bank = ps[:, 4 + group[0] % 4, :].rearrange("p (t n) -> p t n", n=P)
                            cols = slice(tt * P, (tt + 1) * P)
                            if kind == "cmp":
                                act.copy(xT2[0:HD, :, cols], bank[0:HD, :, :])
                                lo = 1 - tt
                                last = act.copy(xT2[HD:P, :, tt * P + lo - 1:(tt + 1) * P - 1], bank[HD:P, :, lo:P])
                            elif kind == "bq":
                                last = act.copy(bqT[:, :, cols], bank)
                            elif kind == "sw":
                                last = act.copy(swT[:, :, cols], bank[:, 0:2, :])
                            elif kind == "hid":
                                kv = tt
                                for m in (0, 1):
                                    src = ps[:, 4 + group[0] % 4, 2 * NBLK * m:2 * NBLK * (m + 1)].rearrange("p (g n) -> p g n", g=2)
                                    dst = hid[:, kv, m, 0:BKV_HEADS, 0:NBLK]
                                    if kv == 1:
                                        dst = hid[:, kv, m, :, 0:NBLK].rearrange("p (g r) n -> p g r n", g=2)
                                        src = src.unsqueeze(2).to_broadcast([P, BKV_HEADS, 4, NBLK])
                                    last = act.activation(dst, src, ACT.Gelu_apprx_tanh,
                                                          bias=ptab[:, T_B1 + 2 * kv + m:T_B1 + 2 * kv + m + 1])
                            elif kind == "cmp2":
                                act.copy(kcn[0:NBLK, 3, :], bank[0:NBLK, 0, :])
                                last = act.copy(vcn[:, :], bank[:, 1, 0:HD])
                            elif kind == "kct":
                                last = act.copy(kcT[:, 0:NBLK], bank[:, 0, 0:NBLK])
                            else:
                                last = act.copy(qkT[:, 4 * kind:4 * kind + 4, cols], bank)
                            last.then_inc(zt_evac, 1)
                            group[0] += 1

                act.wait_ge(cb_ready, 1)
                if layer == 0:
                    act.wait_ge(hid_zeroed, 1)
                for place, c in enumerate(Z_PLACES):
                    if c == "cmp":
                        ahead(layer, ("cmp", 1, 1))
                        used(layer, ("cmp", 1, 1))
                        act.copy(hidn[:, :, :], ps[0:2 * NBLK, 0:2, 0:CMP_HID]).then_inc(z_evac, 1)
                        turn_evac(place - 1)
                        continue
                    for half in (0, 1):
                        ahead(layer, ("z", c, half))
                    used(layer, ("z", c, 1))
                    if place in STAGING_FREE:
                        act.wait_ge(zt_turned, zt + STAGING_FREE[place])
                    pair = ps[:, 2 * (place % 2):2 * (place % 2) + 2, :]
                    st = staging[:, place % 2, :, :]
                    if c < 3:
                        last = act.copy(st, pair)
                    elif c == 3:
                        last = act.copy(va[:, :, 0:512], pair)
                    elif c == 4:
                        act.copy(va[:, :, 512:768], pair[:, :, 0:256])
                        last = act.copy(st[:, :, 0:256], pair[:, :, 256:512])
                    elif c == 5:
                        act.copy(st[:, :, 0:256], pair[:, :, 0:256])
                        for tt in range(TT):
                            src = pair[:, tt, 256:512].rearrange("p (g d) -> p g d", d=HD)
                            for twice in (0, 1):
                                last = act.copy(cmpx[:, tt, :, twice, :], src)
                    else:
                        for tt in range(TT):
                            src = pair[:, tt, :].rearrange("p (b v n) -> p b v n", b=2, v=2)
                            act.copy(st[:, tt, 0:256].rearrange("p (b n) -> p b n", b=2), src[:, :, 0, :])
                            last = act.copy(bv[:, tt, :, :], src[:, :, 1, :])
                    last.then_inc(z_evac, 1)
                    turn_evac(place - 1)
                    if place == 2:
                        act.wait_ge(blkf_ready, 2 * (layer + 1))
                        act.copy(blk_hi[:, :, :, :], blkf[:, :, :, :]).then_inc(blk_hi_ready, 1)
                ahead(layer, ("bg",))
                used(layer, ("bg",))
                act.activation(bgt[:, :, :], ps[:, 0:2, 0:N_BG], ACT.Tanh, scale=0.5).then_inc(z_evac, 1)
                turn_evac(7)

                def exponentials(i):
                    kind, heads, tt = ITEMS[i]
                    c0, n, at = stat_column(i), layer * NI + i, score_at(i)
                    act.wait_ge(shift_ready, n + 1)
                    if i >= 2:
                        act.wait_ge(probT_done, n - 1)
                    wd = item_width(tt)
                    if kind == "A":
                        last = act.activation(prob[:, i % 2, 0:3 * wd], flat[:, at:at + 3 * wd], ACT.Exp, scale=SCALE,
                                              bias=stat[:, 1, c0:c0 + 1], accum_out=stat[:, 2, c0:c0 + 1])
                    elif kind == "B":
                        for r in range(item_rows(ITEMS[i])):
                            last = act.activation(prob[:, i % 2, r * wd:(r + 1) * wd], flat[:, at + r * wd:at + (r + 1) * wd],
                                                  ACT.Exp, scale=SCALE, bias=stat[:, 1, c0 + r:c0 + r + 1],
                                                  accum_out=stat[:, 2, c0 + r:c0 + r + 1])
                    else:
                        last = act.activation(prob[:, i % 2, 0:P], cs[:, :, :].rearrange("p h n -> p (h n)"), ACT.Exp, scale=SCALE)
                    last.then_inc(exp_done, 1)

                exponentials(0)
                for i in range(NI):
                    if i + 1 < NI:
                        exponentials(i + 1)
                    if i < FIRST_GATE:
                        ahead(layer, ("xkv", i // 2))
                        if i == FIRST_GATE - 1:
                            used(layer, ("xkv", 1))
                            act.copy(xkT[:, :, :], ps[:, 0, :].rearrange("p (t n) -> p t n", t=2))
                            act.copy(xv[:, :, :], ps[:, 1, :].rearrange("p (t n) -> p t n", t=2)).then_inc(xkv_ready, 1)
                    elif i < FIRST_GATE + 16:
                        q = i - FIRST_GATE
                        if q % 2 == 0:
                            ahead(layer, ("gate", q // 4, q // 2 % 2))
                        if q % 4 == 3:
                            used(layer, ("gate", q // 4, 1))
                            act.activation(gates[:, q // 4, :, :], ps[:, 0:2, :], ACT.Tanh, scale=0.5).then_inc(z_evac, 1)

                ahead(layer, ("wa",))
                for g in range(3):
                    act.wait_ge(yT_done, layer * PER["yt"] + g + 1)
                    act.copy(yT_hi[:, 2 * g:2 * g + 2, :], ps[:, 4 + g, :].rearrange("p (t n) -> p t n", t=2)).then_inc(yT_hi_ready, 1)
                ahead(layer, ("wb", 0))
                ahead(layer, ("wb", 1))
                for n in (0, 1):
                    for tt in range(TT):
                        hT_high(HT0 + layer * PER["ht"] + 2 * n + tt, 2 * n + tt, hT_hi, 4 * n, tt, scale=0.5)
                for n in (0, 1):
                    for half in (0, 1):
                        ahead(layer, ("mix", n, half))
                layer_norm_high(layer, 0)

                ahead(layer, ("xq",))
                used(layer, ("xq",))
                act.copy(xqT[:, :, :], ps[:, 0, :].rearrange("p (t n) -> p t n", t=2)).then_inc(xq_ready, 1)
                for x in range(4):
                    n = layer * PER["x"] + x
                    act.wait_ge(x_shift, n + 1)
                    if x >= 2:
                        act.wait_ge(x_turned, n - 1)
                    for p in (0, 1):
                        last = act.activation(xprob[:, x % 2, p * S:(p + 1) * S], ps[:, 2 * (x % 2) + p, 0:S], ACT.Exp,
                                              scale=SCALE, bias=xstat[:, 1, 2 * x + p:2 * x + p + 1],
                                              accum_out=xstat[:, 2, 2 * x + p:2 * x + p + 1])
                    last.then_inc(x_exp, 1)
                act.wait_ge(xoT_done, layer + 1)
                act.copy(xoT_hi[:, :, :], ps[:, 1, :].rearrange("p (t n) -> p t n", t=2)).then_inc(xoT_hi_ready, 1)
                ahead(layer, ("xo",))
                layer_norm_high(layer, 1)

                for it in range(FF_IT):
                    cn, fn = layer * PER["conv"] + 2 * it, layer * PER["ffn"] + it
                    for ag, name in enumerate(("ua", "ug")):
                        ahead(layer, (name, it))
                        used(layer, (name, it))
                        if ag == 0 and it >= 2:
                            act.wait_ge(hidf_ready, fn - 1)
                        for j in (0, 1):
                            t = 22 * ag + 2 * it + j
                            last = act.activation(conv_y[:, it % 2, ag, j, :], ps[:, 4 + 2 * (it % 2) + ag, j * S:(j + 1) * S],
                                                  ACT.Identity, scale=ptab[:, T_CONV + 88 + t:T_CONV + 89 + t],
                                                  bias=ptab[:, T_CB + t:T_CB + t + 1])
                        last.then_inc(conv_first, 1)
                    act.wait_ge(conv_done, cn + 1)
                    if it:
                        act.wait_ge(hidf_ready, fn)
                    act.activation(gelu_a[:, :, :], conv_y[:, it % 2, 0, :, :], ACT.Gelu_apprx_tanh).then_inc(gelu_done, 1)
                    if it:
                        ahead(layer, ("down", it - 1))
                    act.wait_ge(hidf_ready, fn + 1)
                    if it >= 2:
                        used(layer, ("down", it - 2))
                    act.copy(hid_hi[:, it % 2, :, :], hidf[:, :, :]).then_inc(hid_hi_ready, 1)
                ahead(layer, ("down", FF_IT - 1))
                if layer < DEPTH - 1:
                    layer_norm_high(layer, 2)

        @block.vector
        def _(dve):
            done = [0]
            steps = [0]
            rope_count = [0]

            def step(ins):
                steps[0] += 1
                ins.then_inc(dve_step, 1)

            def settle():
                dve.wait_ge(dve_step, steps[0])

            def split_through(n):
                while done[0] <= n and done[0] < DEPTH * NU:
                    k = done[0]
                    dve.wait_ge(hi_split, k + 1)
                    size = KT * N_BG if UNITS[k % NU] == ("bg",) else UNIT
                    dve.tensor_tensor(w_lo[:, k % SPLIT, 0:size], raw[:, k % RAW, 0:size],
                                      w_hi[:, k % SPLIT, 0:size].bitcast(F32), ALU.subtract).then_inc(lo_split, 1)
                    done[0] += 1

            def ahead(layer, name):
                split_through(layer * NU + UNIT_AT[name] + SPLIT - 1)

            def hT_low(group, bank, hi, lo, tile0, tt, scale=None):
                cols = slice(tt * P, (tt + 1) * P)
                high = hi[:, tile0:tile0 + 4, cols].bitcast(F32)
                src = ps[:, bank, :].rearrange("p (t n) -> p t n", n=P)
                dve.wait_ge(hT_hi_ready, group + 1)
                if scale is None:
                    last = dve.tensor_tensor(lo[:, tile0:tile0 + 4, cols], src, high, ALU.subtract)
                else:
                    last = dve.scalar_tensor_tensor(out=lo[:, tile0:tile0 + 4, cols], in0=src, scalar=scale, in1=high,
                                                    op0=ALU.mult, op1=ALU.subtract)
                last.then_inc(hT_lo_ready, 1)

            def layer_norm(layer, k, last_unit):
                for tt in range(TT):
                    if tt == 0:
                        dve.wait_ge(res_done, 3 * layer + k + 1)
                    else:
                        dve.wait_ge(unit_used, layer * NU + UNIT_AT[last_unit] + 1)
                    ht = h[:, tt, :]
                    step(dve.scalar_tensor_tensor(out=ht, in0=ht, scalar=ALPHA, in1=flat[:, 1024 * tt:1024 * (tt + 1)],
                                                  op0=ALU.mult, op1=ALU.add))
                    settle()
                    for c in (0, 1):
                        step(dve.bn_stats(lnst[:, tt, c, :], h[:, tt, 512 * c:512 * (c + 1)]))
                    settle()
                    step(dve.bn_aggr(lnmv[:, tt, :], lnst[:, tt, :, :].rearrange("p a b -> p (a b)")))
                    settle()
                    v, r, a, b = (lnv[:, tt, i:i + 1] for i in range(4))
                    step(dve.tensor_scalar(v, lnmv[:, tt, 1:2], LN_EPS, None, ALU.add))
                    settle()
                    step(dve.tensor_scalar(a.bitcast(I32), v.bitcast(I32), 1, None, ALU.logical_shift_right))
                    settle()
                    step(dve.tensor_scalar(r.bitcast(I32), a.bitcast(I32), -1.0, float(0x5F3759DF), ALU.mult, ALU.add))
                    settle()
                    for _ in range(3):
                        step(dve.scalar_tensor_tensor(out=a, in0=r, scalar=v, in1=r, op0=ALU.mult, op1=ALU.mult))
                        settle()
                        step(dve.tensor_scalar(b, a, -0.5, 1.5, ALU.mult, ALU.add))
                        settle()
                        step(dve.tensor_tensor(r, r, b, ALU.mult))
                        settle()
                    step(dve.tensor_scalar(ht, ht, lnmv[:, tt, 0:1], r, ALU.subtract, ALU.mult))
                    settle()
                    dve.wait_ge(gb_loaded, 32 * (3 * layer + k + 1))
                    step(dve.tensor_tensor(ht, ht, gb[:, 0, :], ALU.mult))
                    settle()
                    dve.tensor_tensor(ht, ht, gb[:, 1, :], ALU.add).then_inc(ln_done, 1)
                if k == 2 and layer == DEPTH - 1:
                    return
                for tt in range(TT):
                    for half in (0, 1):
                        hT_low(HT0 + layer * PER["ht"] + 4 * (k + 1) + 2 * tt + half, 4 + 2 * tt + half, hT_hi, hT_lo, 4 * half, tt)

            for g in range(4):
                hT_low(g, g, memT_hi, memT_lo, 4 * (g % 2), g // 2)
            split_through(2)
            for g in range(4):
                hT_low(4 + g, 4 + g, hT_hi, hT_lo, 4 * (g % 2), g // 2)
            dve.wait_ge(const_loaded, 32)

            for layer in range(DEPTH):
                base = layer * PER["z_evac"]
                zt = layer * PER["zt"]

                def rope(place, n_heads):
                    dve.wait_ge(z_evac, base + place + 1)
                    if rope_count[0]:
                        dve.wait_ge(roped, rope_count[0])
                    rope_count[0] += 1
                    n = HD * n_heads
                    heads = lambda t: t.rearrange("p t (g d) -> p t g d", d=HD)
                    x = heads(staging[:, place % 2, :, 0:n])
                    ta, tb = heads(rope_a[:, :, 0:n]), heads(rope_b[:, :, 0:n])
                    table = lambda at: cf[:, at:at + TT * HD].rearrange("p (t d) -> p t d", t=TT)
                    cos = table(F_COS).unsqueeze(2).to_broadcast([P, TT, n_heads, HD])
                    sin = table(F_SIN).unsqueeze(2).to_broadcast([P, TT, n_heads, HD])
                    step(dve.tensor_tensor(ta, x, cos, ALU.mult))
                    half = HD // 2
                    step(dve.tensor_tensor(tb[:, :, :, 0:half], x[:, :, :, half:HD], sin[:, :, :, 0:half], ALU.mult))
                    step(dve.tensor_tensor(tb[:, :, :, half:HD], x[:, :, :, 0:half], sin[:, :, :, half:HD], ALU.mult))
                    settle()
                    if place < 2:
                        for tt in range(TT):
                            pairs = staging[:, 0, tt, :].rearrange("p (j a d) -> p j a d", a=2, d=HD)
                            last = dve.tensor_tensor(pairs[:, :, place, :], ta[:, tt], tb[:, tt], ALU.add)
                            if tt == 0:
                                step(last)
                    else:
                        last = dve.tensor_tensor(x, ta, tb, ALU.add)
                    last.then_inc(roped, 1)

                for place, c in enumerate(Z_PLACES):
                    if c == "cmp":
                        ahead(layer, ("cmp", 1, 1))
                        continue
                    for half in (0, 1):
                        ahead(layer, ("z", c, half))
                    if place == 2:
                        dve.wait_ge(ptab_ready, layer + 1)
                        dve.wait_ge(zt_evac, zt + groups_until("cmp"))
                        for kv in (0, 1):
                            for g in range(BKV_HEADS):
                                src = xT2[:, 2 * kv + g, :].rearrange("p (n j a) -> p j n a", a=2, j=8)
                                for up in (0, 1):
                                    pos = ptab[:, T_POS + 16 * kv + 8 * up:T_POS + 16 * kv + 8 * (up + 1)]
                                    last = dve.tensor_tensor(
                                        blkf[:, kv, 8 * up:8 * (up + 1), NBLK * g:NBLK * (g + 1)],
                                        src[:, :, up:up + NBLK, 0],
                                        pos.unsqueeze(2).to_broadcast([P, 8, NBLK]), ALU.add)
                            last.then_inc(blkf_ready, 1)
                    if c != 3:
                        rope(place, 8 if c < 3 else 4)
                    if place == 2:
                        dve.wait_ge(blk_hi_ready, layer + 1)
                        dve.tensor_tensor(blk_lo[:, :, :, :].rearrange("p v j n -> p (v j n)"),
                                          blkf[:, :, :, :].rearrange("p v j n -> p (v j n)"),
                                          blk_hi[:, :, :, :].rearrange("p v j n -> p (v j n)").bitcast(F32),
                                          ALU.subtract).then_inc(blk_lo_ready, 1)
                    if place == 6:
                        dve.wait_ge(zt_evac, zt + groups_until("cmp2"))
                        k0, k1, k2, kc = (kcn[0:NBLK, m, :].rearrange("p (g d) -> p g d", d=HD) for m in range(4))
                        cos = cf[0:NBLK, F_KC:F_KC + HD].unsqueeze(1).to_broadcast([NBLK, BKV_HEADS, HD])
                        sin = cf[0:NBLK, F_KS:F_KS + HD].unsqueeze(1).to_broadcast([NBLK, BKV_HEADS, HD])
                        half = HD // 2
                        step(dve.tensor_tensor(k1, kc, cos, ALU.mult))
                        step(dve.tensor_tensor(k2[:, :, 0:half], kc[:, :, half:HD], sin[:, :, 0:half], ALU.mult))
                        step(dve.tensor_tensor(k2[:, :, half:HD], kc[:, :, 0:half], sin[:, :, half:HD], ALU.mult))
                        settle()
                        dve.tensor_tensor(k0, k1, k2, ALU.add).then_inc(cmp_vec, 1)
                        dve.tensor_tensor(vcbd[:, :, :], vcn[:, :].unsqueeze(1).to_broadcast([P, BQ_HEADS, HD]),
                                          cf[:, F_BD:F_BD + BQ_HEADS].unsqueeze(2).to_broadcast([P, BQ_HEADS, HD]),
                                          ALU.mult).then_inc(cmp_vec, 1)
                ahead(layer, ("bg",))
                dve.wait_ge(z_evac, base + BG_EVAC)
                step(dve.tensor_scalar(bgt[:, :, :], bgt[:, :, :], 1.0, 0.5, ALU.add, ALU.mult))

                def out_evac(i):
                    kind, heads, tt = ITEMS[i]
                    c0 = stat_column(i)
                    dve.wait_ge(pv_done, layer * NI + i + 1)
                    if kind == "A":
                        last = dve.tensor_scalar(y[:, tt, HD * heads:HD * (heads + 1)], flat[:, OUT:OUT + HD],
                                                 stat[:, 3, c0:c0 + 1], None, ALU.mult)
                    elif kind == "C":
                        last = dve.tensor_tensor(
                            y[:, tt, 256:768].rearrange("p (g d) -> p g d", d=HD),
                            ps[:, 7, :].rearrange("p (g d) -> p g d", d=HD),
                            coef[:, c0:c0 + BQ_HEADS].unsqueeze(2).to_broadcast([P, BQ_HEADS, HD]), ALU.mult)
                    else:
                        dve.wait_ge(o_evac, layer * NI + i)
                        for br in (0, 1):
                            for a, hd in enumerate(heads):
                                r = 2 * a + br
                                yh = y[:, tt, 256 + HD * hd:256 + HD * (hd + 1)]
                                last = dve.scalar_tensor_tensor(out=yh, in0=flat[:, OUT + HD * r:OUT + HD * (r + 1)],
                                                                scalar=coef[:, c0 + r:c0 + r + 1], in1=yh,
                                                                op0=ALU.mult, op1=ALU.add)
                                if br == 0:
                                    step(last)
                            if br == 0:
                                settle()
                    last.then_inc(o_evac, 1)

                def maximum(i):
                    kind, heads, tt = item = ITEMS[i]
                    rows, wd, c0, n, at = item_rows(item), item_width(tt), stat_column(i), layer * NI + i, score_at(i)
                    mx, shift = stat[:, 0, c0:c0 + rows], stat[:, 1, c0:c0 + rows]
                    dve.wait_ge(scores_done, n + 1)
                    if kind == "A":
                        step(dve.reduce_max(mx, flat[:, at:at + 3 * wd], AX.X))
                    elif kind == "B":
                        step(dve.reduce_max(mx, flat[:, at:at + rows * wd].rearrange("p (r n) -> p r n", r=rows), AX.X))
                    else:
                        compressed = flat[:, at:at + 1024].rearrange("p (v m) -> p v m", v=2)[:, :, 0:64].rearrange(
                            "p v (r n) -> p v r n", n=16)
                        step(dve.tensor_reduce(mx.rearrange("p (v r) -> p v r", v=2), compressed, AX.X, ALU.max))
                    settle()
                    if kind == "C":
                        step(dve.tensor_scalar(shift, mx, FLOOR, None, ALU.max))
                        settle()
                        dve.wait_ge(exp_done, n)
                        dve.tensor_tensor(cs[:, :, :].rearrange("p (v r) n -> p v r n", v=2), compressed,
                                          shift.unsqueeze(2).to_broadcast([P, rows, 16]).rearrange("p (v r) n -> p v r n", v=2),
                                          ALU.subtract).then_inc(shift_ready, 1)
                    else:
                        dve.tensor_scalar(shift, mx, -SCALE, None, ALU.mult).then_inc(shift_ready, 1)

                maximum(0)
                for i, item in enumerate(ITEMS):
                    kind, heads, tt = item
                    rows, c0, n = item_rows(item), stat_column(i), layer * NI + i
                    if i + 1 < NI:
                        maximum(i + 1)
                    if i % 2 and i < FIRST_GATE:
                        ahead(layer, ("xkv", i // 2))
                    elif i % 2 and i < FIRST_GATE + 16:
                        q = i - FIRST_GATE
                        ahead(layer, ("gate", q // 4, q // 2 % 2))
                    if i:
                        settle()
                        out_evac(i - 1)
                    dve.wait_ge(exp_done, n + 1)
                    lsum, rsum = stat[:, 2, c0:c0 + rows], stat[:, 3, c0:c0 + rows]
                    if kind == "C":
                        step(dve.reduce_sum(lsum, prob[:, i % 2, 0:P].rearrange("p (r n) -> p r n", r=rows), AX.X))
                        settle()
                        step(dve.tensor_scalar(lsum, lsum, 1e-30, None, ALU.max))
                        settle()
                    step(dve.reciprocal(rsum, lsum))
                    if kind != "A":
                        settle()
                        gate = bgt[:, tt, :].rearrange("p (g b) -> p g b", b=3)
                        if kind == "C":
                            step(dve.tensor_tensor(coef[:, c0:c0 + rows], rsum, gate[:, :, 0], ALU.mult))
                        else:
                            h0, nh = heads[0], len(heads)
                            step(dve.tensor_tensor(coef[:, c0:c0 + rows].rearrange("p (g b) -> p g b", b=2),
                                                   rsum.rearrange("p (g b) -> p g b", b=2), gate[:, h0:h0 + nh, 1:3], ALU.mult))
                    nb = item_blocks(item)
                    dve.wait_ge(probT_done, n + 1)
                    if i >= 2:
                        dve.wait_ge(pv_done, n - 1)
                    dve.tensor_copy(probT[:, i % 2, 0:P * nb], flat[:, TURNED:TURNED + P * nb]).then_inc(probT_evac, 1)
                settle()
                out_evac(NI - 1)

                ahead(layer, ("wa",))
                for g in range(3):
                    dve.wait_ge(yT_hi_ready, layer * PER["yt"] + g + 1)
                    dve.tensor_tensor(yT_lo[:, 2 * g:2 * g + 2, :], ps[:, 4 + g, :].rearrange("p (t n) -> p t n", t=2),
                                      yT_hi[:, 2 * g:2 * g + 2, :].bitcast(F32), ALU.subtract).then_inc(yT_lo_ready, 1)
                ahead(layer, ("wb", 0))
                ahead(layer, ("wb", 1))
                dve.wait_ge(unit_used, layer * NU + UNIT_AT[("wa",)] + 1)
                for n in (0, 1):
                    last = dve.scalar_tensor_tensor(out=gates[:, n, :, :], in0=gates[:, n, :, :], scalar=1.0,
                                                    in1=ps[:, 4 * n:4 * n + 2, :], op0=ALU.add, op1=ALU.mult)
                    last.then_inc(a_gated, 1)
                for n in (0, 1):
                    dve.wait_ge(unit_used, layer * NU + UNIT_AT[("wb", n)] + 1)
                    step(dve.scalar_tensor_tensor(out=gates[:, 2 + n, :, :], in0=gates[:, 2 + n, :, :], scalar=1.0,
                                                  in1=ps[:, 4 * n + 2:4 * n + 4, :], op0=ALU.add, op1=ALU.mult))
                    settle()
                    dve.wait_ge(a_gated, 2 * (layer + 1))
                    dve.tensor_tensor(gates[:, n, :, :], gates[:, n, :, :], gates[:, 2 + n, :, :], ALU.add).then_inc(merged, 1)
                for n in (0, 1):
                    for tt in range(TT):
                        hT_low(HT0 + layer * PER["ht"] + 2 * n + tt, 2 * n + tt, hT_hi, hT_lo, 4 * n, tt, scale=0.5)
                for n in (0, 1):
                    for half in (0, 1):
                        if (n, half) == (0, 0):
                            ahead(layer, ("mix", n, half))
                layer_norm(layer, 0, ("mix", 1, 1))
                ahead(layer, ("mix", 1, 1))

                ahead(layer, ("xq",))
                for x in range(5):
                    n = layer * PER["x"] + x
                    if x < 4:
                        tt, j = x // 2, x % 2
                        mx, shift = xstat[:, 0, 2 * x:2 * x + 2], xstat[:, 1, 2 * x:2 * x + 2]
                        dve.wait_ge(x_scores, n + 1)
                        step(dve.reduce_max(mx, ps[:, 2 * (x % 2):2 * (x % 2) + 2, 0:S], AX.X))
                        settle()
                        dve.tensor_scalar(shift, mx, -SCALE, None, ALU.mult).then_inc(x_shift, 1)
                        dve.wait_ge(x_exp, n + 1)
                        step(dve.reciprocal(xstat[:, 3, 2 * x:2 * x + 2], xstat[:, 2, 2 * x:2 * x + 2]))
                        dve.wait_ge(x_turned, n + 1)
                        if x >= 2:
                            dve.wait_ge(x_pv, n - 1)
                        else:
                            dve.wait_ge(pv_done, NI * (layer + 1))
                        dve.tensor_copy(probT[:, x % 2, 0:512], ps[:, 4 + x % 2, :]).then_inc(x_probT, 1)
                    if x:
                        px = x - 1
                        ptt, pj = px // 2, px % 2
                        settle()
                        dve.wait_ge(x_pv, n)
                        dve.tensor_tensor(xo_n[:, ptt, P * pj:P * (pj + 1)].rearrange("p (g d) -> p g d", d=HD),
                                          ps[:, 6 + px % 2, 0:P].rearrange("p (g d) -> p g d", d=HD),
                                          xstat[:, 3, 2 * px:2 * px + 2].unsqueeze(2).to_broadcast([P, 2, HD]),
                                          ALU.mult).then_inc(x_evac, 1)
                dve.wait_ge(xoT_hi_ready, layer + 1)
                dve.tensor_tensor(xoT_lo[:, :, :], ps[:, 1, :].rearrange("p (t n) -> p t n", t=2),
                                  xoT_hi[:, :, :].bitcast(F32), ALU.subtract).then_inc(xoT_lo_ready, 1)
                layer_norm(layer, 1, ("xo",))
                ahead(layer, ("xo",))

                for it in range(FF_IT):
                    cn, fn = layer * PER["conv"] + 2 * it, layer * PER["ffn"] + it
                    for ag, name in enumerate(("ua", "ug")):
                        ahead(layer, (name, it))
                        dve.wait_ge(conv_first, cn + ag + 1)
                        for back in (1, 2):
                            for j in (0, 1):
                                t = 22 * ag + 2 * it + j
                                tap = ptab[:, T_CONV + 44 * (2 - back) + t:T_CONV + 44 * (2 - back) + t + 1]
                                acc = conv_y[:, it % 2, ag, j, back:S]
                                last = dve.scalar_tensor_tensor(
                                    out=acc, in0=ps[:, 4 + 2 * (it % 2) + ag, j * S:(j + 1) * S - back],
                                    scalar=tap, in1=acc, op0=ALU.mult, op1=ALU.add)
                                if back == 1:
                                    step(last)
                            if back == 1:
                                settle()
                        last.then_inc(conv_done, 1)
                    dve.wait_ge(gelu_done, fn + 1)
                    dve.wait_ge(conv_done, cn + 2)
                    dve.tensor_tensor(hidf[:, :, :], gelu_a[:, :, :], conv_y[:, it % 2, 1, :, :], ALU.mult).then_inc(hidf_ready, 1)
                    if it:
                        ahead(layer, ("down", it - 1))
                    dve.wait_ge(hid_hi_ready, fn + 1)
                    dve.wait_ge(hidf_ready, fn + 1)
                    dve.tensor_tensor(hid_lo[:, it % 2, :, :], hidf[:, :, :], hid_hi[:, it % 2, :, :].bitcast(F32),
                                      ALU.subtract).then_inc(hid_lo_ready, 1)
                ahead(layer, ("down", FF_IT - 1))
                layer_norm(layer, 2, ("down", FF_IT - 1))

        @block.tensor
        def _(pe):
            def product(dst, s_hi, s_lo, m_hi, m_lo, start, stop):
                pe.matmul(dst, s_hi, m_hi, start=start, stop=False, skip_group_check=True)
                pe.matmul(dst, s_hi, m_lo, start=False, stop=False, skip_group_check=True)
                return pe.matmul(dst, s_lo, m_hi, start=False, stop=stop, skip_group_check=True)

            def take(layer, name):
                n = layer * NU + UNIT_AT[name]
                pe.wait_ge(lo_split, n + 1)
                return unit_view(w_hi, n % SPLIT, name), unit_view(w_lo, n % SPLIT, name)

            def turn(group_sem, bank, sources):
                for b, src in enumerate(sources):
                    last = pe.transpose(ps[:, bank, b * P:(b + 1) * P], src, ident)
                last.then_inc(group_sem, 1)

            def turn_h(tt, half, bank):
                turn(hT_turned, bank, [h[:, tt, 512 * half + P * b:512 * half + P * (b + 1)] for b in range(4)])

            def layer_norm_turn(layer, k):
                for tt in range(TT):
                    pe.wait_ge(ln_done, layer * PER["ln"] + 2 * k + tt + 1)
                    for half in (0, 1):
                        turn_h(tt, half, 4 + 2 * tt + half)

            def columns(layer, name, halves, bank0, width, k_of, k_stop):
                whi, wlo = take(layer, name)
                for kk in halves:
                    k = k_of + kk
                    for tt in range(TT):
                        cols = slice(tt * P, (tt + 1) * P)
                        last = product(ps[:, bank0 + tt, 0:width], hT_hi[:, k, cols], hT_lo[:, k, cols],
                                       whi[:, kk, :], wlo[:, kk, :], k == 0, k == k_stop)
                return last

            pe.wait_ge(const_loaded, 32)
            for n in (0, 1):
                pe.wait_ge(act_in_loaded, 16 * (n + 1))
                for tt in range(TT):
                    for half in (0, 1):
                        turn_h(tt, half, 4 * n + 2 * tt + half)

            for layer in range(DEPTH):
                base = layer * PER["z_evac"]
                zt = layer * PER["zt"]
                ht = HT0 + layer * PER["ht"]

                pe.wait_ge(hT_lo_ready, ht)
                pe.wait_ge(prm_loaded, 80 * (layer + 1))
                for b in range(4):
                    pe.transpose(ps[:, 4, 44 * b:44 * (b + 1)], prm_c[:, b, :], ident[0:44, 0:44])
                for b in (0, 1):
                    pe.transpose(ps[:, 4, T_POS + 16 * b:T_POS + 16 * (b + 1)], prm_p[:, b, :], ident[0:16, 0:16])
                pe.transpose(ps[:, 4, T_B1:T_B1 + 4], prm_b[:, :], ident[0:4, 0:4]).then_inc(prm_turned, 1)

                group = [0]

                def compression_turn(kind, kv, bank):
                    if kind == "hid":
                        pe.wait_ge(z_evac, base + Z_PLACES.index("cmp") + 1)
                        for m in (0, 1):
                            last = pe.transpose(ps[:, bank, 2 * NBLK * m:2 * NBLK * (m + 1)], hidn[:, kv, P * m:P * (m + 1)],
                                                ident[0:2 * NBLK, 0:2 * NBLK])
                    elif kind == "cmp2":
                        pe.wait_ge(zt_evac, zt + groups_until("hid"))
                        for g in range(BKV_HEADS):
                            for m in (0, 1):
                                pe.matmul(ps[0:NBLK, bank, HD * g:HD * (g + 1)], hid[:, 0, m, g, 0:NBLK], w2[:, 0, m, :],
                                          start=(m == 0), stop=(m == 1), skip_group_check=True)
                        for m in (0, 1):
                            rep = hid[:, 1, m, :, :].rearrange("p h n -> p (h n)")
                            last = pe.matmul(ps[:, bank, P:P + HD], rep, w2[:, 1, m, :], start=(m == 0), stop=(m == 1),
                                             skip_group_check=True)
                    else:
                        pe.wait_ge(cmp_vec, 2 * layer + 2)
                        last = pe.transpose(ps[:, bank, 0:NBLK], kcn[0:NBLK, 0, :], ident[0:NBLK, 0:NBLK])
                    last.then_inc(zt_turned, 1)

                def z_turn(place):
                    for kind in Z_GROUPS.get(place, ()):
                        for tt in range(TT if kind in TWO else 1):
                            bank = 4 + group[0] % 4
                            if group[0] == 0:
                                pe.wait_ge(ptab_ready, layer + 1)
                                pe.wait_ge(z_evac, base + 2)
                            if kind in ROPES_BEFORE:
                                pe.wait_ge(roped, layer * PER["roped"] + ROPES_BEFORE[kind])
                            if group[0] >= 4:
                                pe.wait_ge(zt_evac, zt + group[0] - 3)
                            if kind in ("hid", "cmp2", "kct"):
                                compression_turn(kind, tt, bank)
                                group[0] += 1
                                continue
                            if kind == "cmp":
                                src = [cmpx[:, tt, b, :, :].rearrange("p a d -> p (a d)") for b in range(4)]
                            elif kind == "bq":
                                src = [staging[:, 0, tt, P * b:P * (b + 1)] for b in range(4)]
                            elif kind == "sw":
                                src = [staging[:, place % 2, tt, P * b:P * (b + 1)] for b in range(2)]
                            else:
                                src = [staging[:, place % 2, tt, P * b:P * (b + 1)] for b in range(4)]
                            turn(zt_turned, 4 + group[0] % 4, src)
                            group[0] += 1

                for place, c in enumerate(Z_PLACES):
                    if place >= 2:
                        pe.wait_ge(z_evac, base + place - 1)
                    if c == "cmp":
                        pe.wait_ge(blk_lo_ready, layer + 1)
                        for kv in (0, 1):
                            for half in (0, 1):
                                whi, wlo = take(layer, ("cmp", kv, half))
                                for kk in range(8):
                                    k = 8 * half + kk
                                    last = product(ps[0:2 * NBLK, kv, 0:CMP_HID], blk_hi[:, kv, k, :], blk_lo[:, kv, k, :],
                                                   whi[:, kk, :], wlo[:, kk, :], k == 0, k == 15)
                                last.then_inc(unit_used, 1)
                        z_turn(place - 1)
                        continue
                    for half in (0, 1):
                        columns(layer, ("z", c, half), range(4), 2 * (place % 2), 512, 4 * half, 7).then_inc(unit_used, 1)
                    z_turn(place - 1)
                pe.wait_ge(z_evac, base + len(Z_PLACES) - 1)
                columns(layer, ("bg",), range(8), 0, N_BG, 0, 7).then_inc(unit_used, 1)
                z_turn(7)

                def scores(i):
                    kind, heads, tt = ITEMS[i]
                    wd, at = item_width(tt), score_at(i)
                    q = slice(tt * P, (tt + 1) * P)
                    if i == 0:
                        pe.wait_ge(cb_ready, 1)
                        pe.wait_ge(z_evac, base + len(Z_PLACES))
                        pe.wait_ge(zt_evac, zt + Z_T)
                    elif i >= 2:
                        pe.wait_ge(exp_done, layer * NI + i - 1)
                    if kind == "A":
                        mask = B_A0 if tt == 0 else B_A1
                        for c in range(0, 3 * wd, 512):
                            n = min(512, 3 * wd - c)
                            pe.matmul(flat[:, at + c:at + c + n], identb, cb[:, mask + c:mask + c + n],
                                      start=True, stop=False, skip_group_check=True)
                        for g in range(A_GROUPS):
                            head = A_HPG * g + heads
                            part = slice(HD * (head % 2), HD * (head % 2) + HD)
                            last = pe.matmul(flat[:, at + g * wd:at + (g + 1) * wd], qkT[part, head // 2, q],
                                             qkT[part, 6 + head // 2, 0:wd], start=False, stop=True, skip_group_check=True)
                    elif kind == "B":
                        mask = B_B0 if tt == 0 else B_B1
                        rows = item_rows(ITEMS[i])
                        pe.matmul(flat[:, at:at + rows * wd], identb,
                                  cb[:, mask:mask + wd].unsqueeze(1).to_broadcast([P, rows, wd]),
                                  start=True, stop=False, skip_group_check=True)
                        for a, hd in enumerate(heads):
                            kv = hd // 4
                            part = slice(HD * kv, HD * kv + HD)
                            for br in (0, 1):
                                r = 2 * a + br
                                last = pe.matmul(flat[:, at + r * wd:at + (r + 1) * wd], bqT[part, hd % 4, q],
                                                 swT[part, br, 0:wd], start=False, stop=True, skip_group_check=True)
                    else:
                        mask = B_C + 16 * tt
                        for kv in range(BKV_HEADS):
                            pe.matmul(ps[:, at // 512 + kv, 0:64], identb,
                                      cb[:, mask:mask + 16].unsqueeze(1).to_broadcast([P, 4, 16]),
                                      start=True, stop=False, skip_group_check=True)
                        for hd in range(BQ_HEADS):
                            part = slice(HD * (hd // 4), HD * (hd // 4) + HD)
                            last = pe.matmul(ps[:, at // 512 + hd // 4, 16 * (hd % 4):16 * (hd % 4) + NBLK], bqT[part, hd % 4, q],
                                             kcT[part, 0:NBLK], start=False, stop=True, skip_group_check=True)
                    last.then_inc(scores_done, 1)

                def filler(i):
                    if i == 0:
                        pe.wait_ge(z_evac, base + BG_EVAC)
                    if i < FIRST_GATE:
                        whi, wlo = take(layer, ("xkv", i // 2))
                        for kk in range(2 * (i % 2), 2 * (i % 2) + 2):
                            k = 4 * (i // 2) + kk
                            for j in (0, 1):
                                cols = slice(j * P, (j + 1) * P)
                                product(ps[:, 0, S * j:S * (j + 1)], whi[:, kk, cols], wlo[:, kk, cols],
                                        memT_hi[:, k, :], memT_lo[:, k, :], k == 0 and j == 0, k == 7)
                            for j in (0, 1):
                                cols = slice(j * P, (j + 1) * P)
                                last = product(ps[:, 1, S * j:S * (j + 1)], memT_hi[:, k, cols], memT_lo[:, k, cols],
                                               whi[:, kk, S:2 * S], wlo[:, kk, S:2 * S], k == 0 and j == 0, k == 7)
                        if i % 2:
                            last.then_inc(unit_used, 1)
                    elif i < FIRST_GATE + 16:
                        q = i - FIRST_GATE
                        c, half = q // 4, q // 2 % 2
                        if q == 0:
                            pe.wait_ge(xkv_ready, layer + 1)
                        elif q % 4 == 0:
                            pe.wait_ge(z_evac, base + BG_EVAC + c)
                        two = range(2 * (q % 2), 2 * (q % 2) + 2)
                        last = columns(layer, ("gate", c, half), two, 0, 512, 4 * half, 7)
                        if q % 2:
                            last.then_inc(unit_used, 1)

                def prob_turn(i):
                    pe.wait_ge(exp_done, layer * NI + i + 1)
                    if i:
                        pe.wait_ge(probT_evac, layer * NI + i)
                    for b in range(item_blocks(ITEMS[i])):
                        if b == 4:
                            pe.wait_ge(o_evac, layer * NI + i)
                        last = pe.transpose(flat[:, TURNED + P * b:TURNED + P * (b + 1)], prob[:, i % 2, P * b:P * (b + 1)], ident)
                    last.then_inc(probT_done, 1)

                def values(i):
                    kind, heads, tt = ITEMS[i]
                    pe.wait_ge(probT_evac, layer * NI + i + 1)
                    if i:
                        pe.wait_ge(o_evac, layer * NI + i)
                    blocks = tt + 1
                    if kind == "A":
                        for g in range(A_GROUPS):
                            head = A_HPG * g + heads
                            for kt in range(blocks):
                                b = g * blocks + kt
                                last = pe.matmul(flat[:, OUT:OUT + HD], probT[:, i % 2, P * b:P * (b + 1)],
                                                 va[:, kt, HD * head:HD * (head + 1)], start=(b == 0),
                                                 stop=(b == 3 * blocks - 1), skip_group_check=True)
                    elif kind == "B":
                        for a, hd in enumerate(heads):
                            kv = hd // 4
                            for br in (0, 1):
                                r = 2 * a + br
                                for kt in range(blocks):
                                    b = r * blocks + kt
                                    last = pe.matmul(flat[:, OUT + HD * r:OUT + HD * (r + 1)], probT[:, i % 2, P * b:P * (b + 1)],
                                                     bv[:, kt, br, HD * kv:HD * (kv + 1)], start=(kt == 0),
                                                     stop=(kt == blocks - 1), skip_group_check=True)
                    else:
                        last = pe.matmul(ps[:, 7, :], probT[:, i % 2, 0:P], vcbd[:, :, :].rearrange("p g d -> p (g d)"),
                                         start=True, stop=True)
                    last.then_inc(pv_done, 1)

                scores(0)
                for i in range(NI):
                    if i + 1 < NI:
                        scores(i + 1)
                    if i:
                        values(i - 1)
                    filler(i)
                    prob_turn(i)
                values(NI - 1)

                pe.wait_ge(o_evac, NI * (layer + 1))
                for g in range(3):
                    turn(yT_done, 4 + g, [y[:, tt, P * (2 * g + t):P * (2 * g + t + 1)] for t in (0, 1) for tt in range(TT)])

                pe.wait_ge(z_evac, base + PER["z_evac"])
                pe.wait_ge(yT_lo_ready, layer * PER["yt"] + 3)

                def branch(whi, wlo, tile0, n_tiles, col, bank0):
                    for k in range(n_tiles):
                        for tt in range(TT):
                            cols = slice(tt * P, (tt + 1) * P)
                            last = product(ps[:, bank0 + tt, :], yT_hi[:, tile0 + k, cols], yT_lo[:, tile0 + k, cols],
                                           whi[:, k, col:col + 512], wlo[:, k, col:col + 512], k == 0, k == n_tiles - 1)
                    return last

                whi, wlo = take(layer, ("wa",))
                branch(whi, wlo, 0, 2, 0, 0)
                branch(whi, wlo, 0, 2, 512, 4).then_inc(unit_used, 1)
                for n in (0, 1):
                    whi, wlo = take(layer, ("wb", n))
                    branch(whi, wlo, 2, 4, 0, 4 * n + 2).then_inc(unit_used, 1)

                for n in (0, 1):
                    pe.wait_ge(merged, 2 * layer + n + 1)
                    for tt in range(TT):
                        turn(hT_turned, 2 * n + tt, [gates[:, n, tt, P * b:P * (b + 1)] for b in range(4)])

                pe.wait_ge(hT_lo_ready, ht + 4)
                for tt in range(TT):
                    cols = slice(tt * P, (tt + 1) * P)
                    for n in (0, 1):
                        for half in (0, 1):
                            whi, wlo = take(layer, ("mix", n, half))
                            for kk in range(4):
                                k = 4 * half + kk
                                last = product(ps[:, 2 * tt + n, :], hT_hi[:, k, cols], hT_lo[:, k, cols],
                                               whi[:, kk, :], wlo[:, kk, :], k == 0, k == 7)
                            if tt == 1:
                                last.then_inc(unit_used, 1)
                    if tt == 0:
                        last.then_inc(res_done, 1)
                layer_norm_turn(layer, 0)

                pe.wait_ge(hT_lo_ready, ht + 8)
                whi, wlo = take(layer, ("xq",))
                for j in (0, 1):
                    for k in range(KT):
                        last = product(ps[:, 0, S * j:S * (j + 1)], whi[:, k, P * j:P * (j + 1)], wlo[:, k, P * j:P * (j + 1)],
                                       hT_hi[:, k, :], hT_lo[:, k, :], k == 0, k == KT - 1)
                last.then_inc(unit_used, 1)
                pe.wait_ge(xq_ready, layer + 1)
                for x in range(6):
                    n = layer * PER["x"] + x
                    if x < 4:
                        tt, j = x // 2, x % 2
                        if x >= 2:
                            pe.wait_ge(x_exp, n - 1)
                        for p in (0, 1):
                            part = slice(HD * p, HD * (p + 1))
                            last = pe.matmul(ps[:, 2 * (x % 2) + p, 0:S], xqT[part, j, tt * P:(tt + 1) * P],
                                             xkT[part, j, :], start=True, stop=True, skip_group_check=True)
                        last.then_inc(x_scores, 1)
                    if 1 <= x < 5:
                        px = x - 1
                        pe.wait_ge(x_exp, n)
                        if px >= 2:
                            pe.wait_ge(x_probT, n - 2)
                        turn(x_turned, 4 + px % 2, [xprob[:, px % 2, P * b:P * (b + 1)] for b in range(4)])
                    if x >= 2:
                        px = x - 2
                        j = px % 2
                        pe.wait_ge(x_probT, n - 1)
                        if px >= 2:
                            pe.wait_ge(x_evac, n - 3)
                        for p in (0, 1):
                            for kt in (0, 1):
                                b = 2 * p + kt
                                last = pe.matmul(ps[:, 6 + px % 2, HD * p:HD * (p + 1)], probT[:, px % 2, P * b:P * (b + 1)],
                                                 xv[:, kt, HD * (2 * j + p):HD * (2 * j + p + 1)], start=(kt == 0),
                                                 stop=(kt == 1), skip_group_check=True)
                        last.then_inc(x_pv, 1)
                pe.wait_ge(x_evac, 4 * (layer + 1))
                turn(xoT_done, 1, [xo_n[:, tt, P * t:P * (t + 1)] for t in (0, 1) for tt in range(TT)])
                pe.wait_ge(xoT_lo_ready, layer + 1)
                whi, wlo = take(layer, ("xo",))
                for tt in range(TT):
                    cols = slice(tt * P, (tt + 1) * P)
                    for n in (0, 1):
                        for k in (0, 1):
                            last = product(ps[:, 2 * tt + n, :], xoT_hi[:, k, cols], xoT_lo[:, k, cols],
                                           whi[:, k, 512 * n:512 * (n + 1)], wlo[:, k, 512 * n:512 * (n + 1)], k == 0, k == 1)
                    last.then_inc(res_done if tt == 0 else unit_used, 1)
                layer_norm_turn(layer, 1)

                pe.wait_ge(hT_lo_ready, ht + 12)

                def down(it):
                    pe.wait_ge(hid_lo_ready, layer * PER["ffn"] + it + 1)
                    whi, wlo = take(layer, ("down", it))
                    for tt in range(TT):
                        cols = slice(tt * P, (tt + 1) * P)
                        for n in (0, 1):
                            for k in (0, 1):
                                last = product(ps[:, 2 * tt + n, :], hid_hi[:, it % 2, k, cols], hid_lo[:, it % 2, k, cols],
                                               whi[:, k, 512 * n:512 * (n + 1)], wlo[:, k, 512 * n:512 * (n + 1)],
                                               it == 0 and k == 0, it == FF_IT - 1 and k == 1)
                        if tt == 1:
                            last.then_inc(unit_used, 1)
                        elif it == FF_IT - 1:
                            last.then_inc(res_done, 1)

                for it in range(FF_IT):
                    for ag, name in enumerate(("ua", "ug")):
                        if it >= 2:
                            pe.wait_ge(conv_done, layer * PER["conv"] + 2 * (it - 2) + ag + 1)
                        whi, wlo = take(layer, (name, it))
                        for j in (0, 1):
                            cols = slice(j * P, (j + 1) * P)
                            for k in range(KT):
                                last = product(ps[:, 4 + 2 * (it % 2) + ag, S * j:S * (j + 1)], whi[:, k, cols], wlo[:, k, cols],
                                               hT_hi[:, k, :], hT_lo[:, k, :], k == 0, k == KT - 1)
                        last.then_inc(unit_used, 1)
                    if it:
                        down(it - 1)
                down(FF_IT - 1)
                if layer < DEPTH - 1:
                    pe.wait_ge(conv_done, PER["conv"] * (layer + 1))
                    layer_norm_turn(layer, 2)


_INS = ["x", "mem", "w_in", "cmp_pos", "cmp_w1", "cmp_b1", "cmp_w2", "w_branch_a", "w_branch_b", "w_mix_out",
        "ln1_g", "ln1_b", "w_xq", "w_xkv", "w_xo", "ln2_g", "ln2_b", "w_up", "conv_w", "conv_b", "w_down",
        "ln3_g", "ln3_b"]


def kernel(**inputs):
    import concourse.bacc as bacc
    from concourse.bass_utils import run_bass_kernel_spmd

    nc = bacc.Bacc("TRN2", target_bir_lowering=False, num_devices=1)
    arrays = {f"in_{name}": np.ascontiguousarray(inputs[name]) for name in _INS}
    arrays["const_f"], arrays["const_b"] = shape_constants()
    aps = {name: nc.dram_tensor(name, list(a.shape), mybir.dt.from_np(a.dtype), kind="ExternalInput").ap()
           for name, a in arrays.items()}
    out = nc.dram_tensor("out", [1, S, D], F32, kind="ExternalOutput").ap()
    hybrid_decoder_kernel(nc, {name: aps[f"in_{name}"] for name in _INS}, aps["const_f"], aps["const_b"], out)
    result = run_bass_kernel_spmd(nc, [arrays], core_ids=[0])
    return result.results[0]["out"]
```

```python
from contextlib import ExitStack

import numpy as np

import concourse.bass as bass
from concourse import mybir

F32 = mybir.dt.float32
F32R = mybir.dt.float32r
BF16 = mybir.dt.bfloat16
I32 = mybir.dt.int32
ACT = mybir.ActivationFunctionType
ALU = mybir.AluOpType
AX = mybir.AxisListType

P = 128
D = 1024
S = 256
TT = S // P
DEPTH = 2
HD = 64
KT = D // P
A_GROUPS, A_HPG = 3, 4
DIL = ((128, 1), (512, 4), (2048, 16))
BQ_HEADS, BKV_HEADS = 8, 2
CMP_STRIDE, CMP_LEN, CMP_HID = 16, 32, 256
NBLK = S // CMP_STRIDE - 1
FF = 2816
X_HEADS = 4
ALPHA = (2 * DEPTH) ** 0.25
LN_EPS = 1e-5
SCALE = HD ** -0.5
NEG = -1e30
FLOOR = -1e29
THETA = 10000.0

COL_BG = 3 * A_GROUPS * A_HPG * HD + BQ_HEADS * HD + 6 * BKV_HEADS * HD
N_BG = 3 * BQ_HEADS
COL_GATE = COL_BG + N_BG

UNIT = 2048
RAW, SPLIT = 3, 4

Z_PLACES = (4, 5, 0, 1, "cmp", 2, 3, 6)
FF_IT = FF // 256


def plan_units(layer):
    u = []
    for c in Z_PLACES:
        if c == "cmp":
            u += [("cmp", kv, half) for kv in (0, 1) for half in (0, 1)]
        else:
            u += [("z", c, half) for half in (0, 1)]
    u += [("bg",)]
    u += [("gate", c, half) for c in range(4) for half in (0, 1)]
    u += [("wa",), ("wb", 0), ("wb", 1)]
    u += [("mix", n, half) for half in (0, 1) for n in (0, 1)]
    if layer == 0:
        u += [("xkv", 0), ("xkv", 1)]
    u += [("xq",), ("xo",)]
    u = [(layer, name) for name in u]
    if layer < DEPTH - 1:
        u += [(layer + 1, ("xkv", half)) for half in (0, 1)]
    for it in range(FF_IT):
        u += [(layer, ("ua", it)), (layer, ("ug", it))]
        if it:
            u += [(layer, ("down", it - 1))]
    return u + [(layer, ("down", FF_IT - 1))]


UNITS = [unit for layer in range(DEPTH) for unit in plan_units(layer)]
NU = len(UNITS)
UNIT_AT = {unit: i for i, unit in enumerate(UNITS)}

ITEMS = [("A", h, tt) for h in range(A_HPG) for tt in range(TT)]
ITEMS += [("C", None, tt) for tt in range(TT)]
ITEMS += [("B", (2 * p, 2 * p + 1), 0) for p in range(BQ_HEADS // 2)]
ITEMS += [("B", (h,), 1) for h in range(BQ_HEADS)]
NI = len(ITEMS)
FIRST_GATE = 2
TURN_A = 12
FILL_WA = NI - 2
assert FIRST_GATE + 16 <= FILL_WA and TURN_A > 2 * A_HPG


def gate_quarter(i):
    q = i - FIRST_GATE
    return q if 0 <= q < 16 else None


Z_GROUPS = {1: ["cmp", "bq"], 2: [0], 3: [1], 4: ["hid"], 5: [2, "cmp2"], 6: ["kct"], 7: ["sw"]}
TWO = ("cmp", "bq", "hid", "sw", 0, 1, 2)
Z_T = sum(2 if kind in TWO else 1 for v in Z_GROUPS.values() for kind in v)


def groups_until(kind):
    n = 0
    for place in sorted(Z_GROUPS):
        for other in Z_GROUPS[place]:
            n += 2 if other in TWO else 1
            if other == kind:
                return n


STAGING_FREE = {2: groups_until("bq"), 3: groups_until("bq"), 5: groups_until(1), 7: groups_until(2)}
ROPES_BEFORE = {"bq": 2, 0: 3, 1: 4, 2: 5, "sw": 6}
BG_EVAC = len(Z_PLACES) + 2

PER = dict(z_evac=BG_EVAC + 4, zt=Z_T, roped=6, item=NI, yt=3, ht=16, ln=12, conv=2 * FF_IT, ffn=FF_IT, x=4)
HT0 = 8


def start_group(layer):
    return HT0 + layer * PER["ht"] - 4 if layer else 0


F_ID, F_COS, F_SIN, F_BD, F_KC, F_KS, F_END = 0, 128, 256, 384, 392, 456, 520
B_ID, B_A0, B_A1, B_B0, B_B1, B_C, B_END = 0, 128, 512, 1280, 1408, 1664, 1696
T_CONV, T_CB, T_POS, T_B1, T_END = 0, 132, 176, 208, 212


def shape_constants():
    half = HD // 2
    inv = (np.float32(THETA) ** (-np.arange(half, dtype=np.float32) / np.float32(half))).astype(np.float32)

    def rope_rows(pos):
        ang = pos.astype(np.float32)[:, None] * inv[None, :]
        c, s = np.cos(ang).astype(np.float32), np.sin(ang).astype(np.float32)
        return np.concatenate([c, c], 1), np.concatenate([-s, s], 1)

    f = np.zeros((P, F_END), np.float32)
    f[:, F_ID:F_ID + P] = np.eye(P)
    for tt in range(TT):
        c, s = rope_rows(np.arange(tt * P, (tt + 1) * P))
        f[:, F_COS + HD * tt:F_COS + HD * (tt + 1)] = c
        f[:, F_SIN + HD * tt:F_SIN + HD * (tt + 1)] = s
    f[np.arange(P), F_BD + np.arange(P) // 16] = 1.0
    c, s = rope_rows(CMP_STRIDE * np.arange(NBLK) + CMP_LEN - 1)
    f[:NBLK, F_KC:F_KC + HD] = c
    f[:NBLK, F_KS:F_KS + HD] = s
    b = np.zeros((P, B_END), np.float32)
    b[:, B_ID:B_ID + P] = np.eye(P)
    for tt, at_a, at_b in ((0, B_A0, B_B0), (1, B_A1, B_B1)):
        w = P * (tt + 1)
        dist = (tt * P + np.arange(P))[:, None] - np.arange(w)[None, :]
        for g, (window, dil) in enumerate(DIL):
            ok = (dist >= 0) & (dist <= window) & (dist % dil == 0)
            b[:, at_a + g * w:at_a + (g + 1) * w] = np.where(ok, 0.0, NEG)
        b[:, at_b:at_b + w] = np.where(dist >= 0, 0.0, NEG)
        ends = CMP_STRIDE * np.arange(16) + CMP_LEN - 1
        ok = (ends[None, :] <= (tt * P + np.arange(P))[:, None]) & (np.arange(16) < NBLK)[None, :]
        b[:, B_C + 16 * tt:B_C + 16 * (tt + 1)] = np.where(ok, 0.0, NEG)
    return f, b


def hybrid_decoder_kernel(nc, w, const_f, const_b, out):
    with ExitStack() as ctx:
        def sb(name, shape, dt=F32):
            return ctx.enter_context(nc.sbuf_tensor(name, shape, dt))

        def sem(name):
            return ctx.enter_context(nc.semaphore(name))

        raw = sb("raw", [P, RAW, UNIT])
        w_hi = sb("w_hi", [P, SPLIT, UNIT], F32R)
        w_lo = sb("w_lo", [P, SPLIT, UNIT], F32R)
        h = sb("h", [P, TT, D])
        hT_hi = sb("hT_hi", [P, KT, S], F32R)
        hT_lo = sb("hT_lo", [P, KT, S], F32R)
        memT_hi = sb("memT_hi", [P, KT, S], F32R)
        memT_lo = sb("memT_lo", [P, KT, S], F32R)
        cf = sb("cf", [P, F_END])
        cb = sb("cb", [P, B_END], BF16)
        ptab = sb("ptab", [P, T_END])
        w2 = sb("w2", [P, 2, 2, HD])
        kcT = sb("kcT", [P, 16])
        cs = sb("cs", [P, BQ_HEADS, 16])
        bgt = sb("bgt", [P, TT, N_BG])
        stat = sb("stat", [P, 4, 64])
        coef = sb("coef", [P, 64])
        xstat = sb("xstat", [P, 4, 8])
        lnst = sb("lnst", [P, TT, 2, 6])
        lnmv = sb("lnmv", [P, TT, 2])
        lnv = sb("lnv", [P, TT, 8])

        def arena(name, size):
            base = nc.sbuf_base
            sb(name, [P, size // 4])

            def at(label, shape, offset, dt=F32):
                return nc.alloc_sbuf_tensor_at(label, shape, dt, offset=base + offset)
            return at

        arena_0 = arena("arena_0", 8192)
        gb = arena_0("gb", [P, 2, D], 0)
        prob = arena_0("prob", [P, 2, 768], 0)
        hidn = arena_0("hidn", [2 * NBLK, 2, CMP_HID], 6144)

        bgn = arena_0("bgn", [N_BG, S], 6144)
        mem_n = arena_0("mem_n", [P, TT, D], 0)

        arena_1 = arena("arena_1", 16384)
        staging = arena_1("staging", [P, 2, TT, 512], 0)
        rope_a = arena_1("rope_a", [P, TT, 512], 8192)
        rope_b = arena_1("rope_b", [P, TT, 512], 12288)
        probT = arena_1("probT", [P, 2, 768], 3072)
        y = arena_1("y", [P, TT, 768], 9216)
        conv_y = arena_1("conv_y", [P, 2, 2, 2, S], 0)
        gelu_a = arena_1("gelu_a", [P, 2, S], 8192)
        hidf = arena_1("hidf", [P, 2, S], 10240)

        arena_2 = arena("arena_2", 16384)
        gates = arena_2("gates", [P, 4, TT, 512], 0)
        cmpx = arena_2("cmpx", [P, TT, 4, 2, HD], 0)
        xT2 = arena_2("xT2", [P, 4, S], 4096)
        hid = arena_2("hid", [P, 2, 2, BQ_HEADS, 16], 4096)
        blk_hi = arena_2("blk_hi", [P, 2, 16, 2 * NBLK], 8192, F32R)
        blk_lo = arena_2("blk_lo", [P, 2, 16, 2 * NBLK], 12288, F32R)
        vcbd = arena_2("vcbd", [P, BQ_HEADS, HD], 8192)
        kcn = arena_2("kcn", [16, 4, P], 10240)
        vcn = arena_2("vcn", [P, HD], 12288)
        xqT = arena_2("xqT", [P, 2, S], 0)
        xprob = arena_2("xprob", [P, 2, 512], 2048)
        xo_n = arena_2("xo_n", [P, TT, S], 6144)
        xoT_hi = arena_2("xoT_hi", [P, 2, S], 8192, F32R)
        xoT_lo = arena_2("xoT_lo", [P, 2, S], 10240, F32R)
        xq_n = arena_2("xq_n", [P, TT, S], 12288)
        hid_hi = arena_2("hid_hi", [P, 2, 2, S], 0, F32R)
        hid_lo = arena_2("hid_lo", [P, 2, 2, S], 4096, F32R)

        arena_3 = arena("arena_3", 12288 + 4096)
        qkT = arena_3("qkT", [P, 12, S], 0)
        const_staged = arena_3("const_staged", [P, B_END], 0)
        blkf = arena_3("blkf", [P, 2, 16, 2 * NBLK], 8192)
        yT_hi = arena_3("yT_hi", [P, 6, S], 0, F32R)
        yT_lo = arena_3("yT_lo", [P, 6, S], 6144, F32R)
        bqT = arena_3("bqT", [P, 4, S], 12288)
        prm_c = arena_3("prm_c", [44, 4, P], 12288)
        prm_p = arena_3("prm_p", [16, 2, P], 12288 + 2048)
        prm_b = arena_3("prm_b", [4, P], 12288 + 3072)

        va = sb("va", [P, TT, 768])
        bv = sb("bv", [P, TT, 2, P])
        swT = sb("swT", [P, 2, S])
        xkT = sb("xkT", [P, 2, S])
        xv = sb("xv", [P, 2, S])

        ps = ctx.enter_context(nc.psum_tensor("ps", [P, 8, 512], F32))
        flat = ps[:, :, :].rearrange("p b n -> p (b n)")

        ident = cf[:, F_ID:F_ID + P]
        identb = cb[:, B_ID:B_ID + P]

        const_loaded = sem("const_loaded")
        masks_loaded = sem("masks_loaded")
        cb_ready = sem("cb_ready")
        x_loaded = [sem(f"x_loaded{i}") for i in range(TT)]
        mem_loaded = sem("mem_loaded")
        raw_loaded = [sem(f"raw_loaded{i}") for i in range(RAW)]
        hi_split = sem("hi_split")
        lo_split = sem("lo_split")
        unit_used = sem("unit_used")
        gb_loaded = sem("gb_loaded")
        prm_loaded = sem("prm_loaded")
        prm_turned = sem("prm_turned")
        ptab_ready = sem("ptab_ready")
        z_evac = sem("z_evac")
        zt_turned = sem("zt_turned")
        zt_evac = sem("zt_evac")
        roped = sem("roped")
        hid_zeroed = sem("hid_zeroed")
        blkf_ready = sem("blkf_ready")
        blk_hi_ready = sem("blk_hi_ready")
        blk_lo_ready = sem("blk_lo_ready")
        cmp_vec = sem("cmp_vec")
        bg_turned = sem("bg_turned")
        scores_done = sem("scores_done")
        shift_ready = sem("shift_ready")
        exp_done = sem("exp_done")
        probT_done = sem("probT_done")
        probT_evac = sem("probT_evac")
        pv_done = sem("pv_done")
        o_evac = sem("o_evac")
        yT_done = sem("yT_done")
        wa_done = sem("wa_done")
        yT_hi_ready = sem("yT_hi_ready")
        yT_lo_ready = sem("yT_lo_ready")
        a_gated = sem("a_gated")
        merged = sem("merged")
        xkv_ready = sem("xkv_ready")
        hT_turned = sem("hT_turned")
        hT_hi_ready = sem("hT_hi_ready")
        hT_lo_ready = sem("hT_lo_ready")
        res_done = sem("res_done")
        ln_done = sem("ln_done")
        xq_done = sem("xq_done")
        xqn_ready = sem("xqn_ready")
        xqT_done = sem("xqT_done")
        xq_ready = sem("xq_ready")
        x_scores = sem("x_scores")
        x_shift = sem("x_shift")
        x_exp = sem("x_exp")
        x_turned = sem("x_turned")
        x_probT = sem("x_probT")
        x_pv = sem("x_pv")
        x_evac = sem("x_evac")
        xoT_done = sem("xoT_done")
        xoT_hi_ready = sem("xoT_hi_ready")
        xoT_lo_ready = sem("xoT_lo_ready")
        conv_first = sem("conv_first")
        conv_done = sem("conv_done")
        gelu_done = sem("gelu_done")
        hidf_ready = sem("hidf_ready")
        hid_hi_ready = sem("hid_hi_ready")
        hid_lo_ready = sem("hid_lo_ready")
        out_stored = sem("out_stored")
        dve_step = sem("dve_step")

        def unit_view(t, slot, name):
            kind = name[0]
            if kind == "bg":
                return t[:, slot, 0:KT * N_BG].rearrange("p (k n) -> p k n", k=KT)
            k = {"z": 4, "gate": 4, "wb": 4, "xkv": 4, "mix": 4, "wa": 2, "xo": 2, "down": 2}.get(kind, 8)
            return t[:, slot, :].rearrange("p (k n) -> p k n", k=k)

        def unit_source(layer, name):
            kind = name[0]
            if kind in ("z", "gate"):
                col = 512 * name[1] + (COL_GATE if kind == "gate" else 0)
                src = w["w_in"][layer, 512 * name[2]:512 * (name[2] + 1), col:col + 512]
            elif kind == "bg":
                src = w["w_in"][layer, :, COL_BG:COL_BG + N_BG]
            elif kind == "cmp":
                src = w["cmp_w1"][layer, name[1], 1024 * name[2]:1024 * (name[2] + 1), :]
            elif kind == "wa":
                src = w["w_branch_a"][layer, :, :]
            elif kind == "wb":
                src = w["w_branch_b"][layer, :, 512 * name[1]:512 * (name[1] + 1)]
            elif kind == "xkv":
                src = w["w_xkv"][layer, 512 * name[1]:512 * (name[1] + 1), :]
            elif kind == "mix":
                src = w["w_mix_out"][layer, 512 * name[2]:512 * (name[2] + 1), 512 * name[1]:512 * (name[1] + 1)]
            elif kind == "xq":
                src = w["w_xq"][layer, :, :]
            elif kind == "xo":
                src = w["w_xo"][layer, :, :]
            elif kind == "ua":
                src = w["w_up"][layer, :, 256 * name[1]:256 * (name[1] + 1)]
            elif kind == "ug":
                src = w["w_up"][layer, :, FF + 256 * name[1]:FF + 256 * (name[1] + 1)]
            else:
                src = w["w_down"][layer, 256 * name[1]:256 * (name[1] + 1), :]
            return src.rearrange("(k p) n -> p k n", p=P)

        def item_width(tt):
            return P * (tt + 1)

        def item_rows(item):
            kind, heads, tt = item
            return 1 if kind == "A" else 2 * len(heads) if kind == "B" else BQ_HEADS

        def item_blocks(item):
            kind, heads, tt = item
            return 1 if kind == "C" else 3 * (tt + 1) if kind == "A" else 4

        def turned_bank(k, tt):
            return 0 if (k, tt) == (1, 1) else 4 + 2 * tt

        def stat_column(i):
            return sum(item_rows(x) for x in ITEMS[:i])

        def score_at(i):
            return 1024 * (1 + i % 2)

        TURNED, OUT = 6 * 512, 7 * 512 + 256

        block = ctx.enter_context(nc.Block())

        @block.sync
        def _(sp):
            def load_x(tt):
                sp.dma_start(h[:, tt, :], w["x"][0, tt * P:(tt + 1) * P, :]).then_inc(x_loaded[tt], 16)

            load_x(0)
            sp.dma_start(cf[:, :], const_f).then_inc(const_loaded, 16)
            for n, (layer, name) in enumerate(UNITS):
                if n >= RAW:
                    sp.wait_ge(lo_split, n - RAW + 1)
                if n == 2:
                    load_x(1)
                if n == 7:
                    sp.dma_start(const_staged[:, :], const_b).then_inc(masks_loaded, 16)
                if n == 5:
                    sp.dma_start(mem_n[:, :, :], w["mem"][0].rearrange("(t p) d -> p t d", p=P)).then_inc(mem_loaded, 16)
                sp.dma_start(unit_view(raw, n % RAW, name), unit_source(layer, name)).then_inc(raw_loaded[n % RAW], 16)
            for tt in range(TT):
                for half in (0, 1):
                    sp.wait_ge(ln_done, DEPTH * PER["ln"] - 2 * TT + 2 * tt + half + 1)
                    cols = slice(512 * half, 512 * (half + 1))
                    sp.dma_start(out[0, tt * P:(tt + 1) * P, cols], h[:, tt, cols]).then_inc(out_stored, 16)
            sp.wait_ge(out_stored, 16 * 2 * TT)

        @block.gpsimd
        def _(pool):
            for layer in range(DEPTH):
                if layer:
                    pool.wait_ge(x_evac, layer * PER["x"])
                t = w["conv_w"][layer].rearrange("i (t p) -> t i p", p=P)
                pool.dma_start(prm_c[:, 0:3, :], t).then_inc(prm_loaded, 16)
                t = w["conv_b"][layer].rearrange("(t p) -> t p", p=P)
                pool.dma_start(prm_c[:, 3, :], t).then_inc(prm_loaded, 16)
                t = w["cmp_pos"][layer].rearrange("v (j a) d -> j v (a d)", a=2)
                pool.dma_start(prm_p[:, :, :], t).then_inc(prm_loaded, 16)
                t = w["cmp_b1"][layer].rearrange("v (m p) -> (v m) p", p=P)
                pool.dma_start(prm_b[:, :], t).then_inc(prm_loaded, 16)
                t = w["cmp_w2"][layer].rearrange("v (m p) d -> p v m d", p=P)
                pool.dma_start(w2[:, :, :, :], t).then_inc(prm_loaded, 16)
                pool.wait_ge(blkf_ready, 2 * (layer + 1))
                pool.memset(hid[:, :, :, :, :], 0.0).then_inc(hid_zeroed, 1)
                for k, (g, b) in enumerate((("ln1_g", "ln1_b"), ("ln2_g", "ln2_b"), ("ln3_g", "ln3_b"))):
                    if k == 0:
                        pool.wait_ge(probT_done, NI * (layer + 1))
                    else:
                        pool.wait_ge(ln_done, layer * PER["ln"] + 4 * k)
                    pool.dma_start(gb[:, 0, :], w[g][layer:layer + 1, :].partition_broadcast(P)).then_inc(gb_loaded, 16)
                    pool.dma_start(gb[:, 1, :], w[b][layer:layer + 1, :].partition_broadcast(P)).then_inc(gb_loaded, 16)

        @block.scalar
        def _(act):
            done = [0]

            def split_through(n):
                while done[0] <= n and done[0] < NU:
                    k = done[0]
                    act.wait_ge(raw_loaded[k % RAW], 16 * (k // RAW + 1))
                    if k >= SPLIT:
                        act.wait_ge(unit_used, k - SPLIT + 1)
                    size = KT * N_BG if UNITS[k][1] == ("bg",) else UNIT
                    act.copy(w_hi[:, k % SPLIT, 0:size], raw[:, k % RAW, 0:size]).then_inc(hi_split, 1)
                    done[0] += 1

            def ahead(layer, name):
                split_through(UNIT_AT[layer, name] + SPLIT - 1)

            def used(layer, name):
                act.wait_ge(unit_used, UNIT_AT[layer, name] + 1)

            def hT_high(group, bank, dst, tile0, tt, scale=1.0):
                act.wait_ge(hT_turned, group + 1)
                act.activation(dst[:, tile0:tile0 + 4, tt * P:(tt + 1) * P],
                               ps[:, bank, :].rearrange("p (t n) -> p t n", n=P),
                               ACT.Identity, scale=scale).then_inc(hT_hi_ready, 1)

            def layer_norm_high(layer, k, tt):
                for half in (0, 1):
                    hT_high(HT0 + layer * PER["ht"] + 4 * (k + 1) + 2 * tt + half, turned_bank(k, tt) + half, hT_hi, 4 * half, tt)

            for g in range(4):
                if g == 2:
                    split_through(SPLIT - 1)
                hT_high(g, 4 + g, hT_hi, 4 * (g % 2), g // 2)

            for layer in range(DEPTH):
                base = layer * PER["z_evac"]
                zt = layer * PER["zt"]
                group = [0]

                def turn_evac(place):
                    for kind in Z_GROUPS.get(place, ()):
                        for tt in range(TT if kind in TWO else 1):
                            act.wait_ge(zt_turned, zt + group[0] + 1)
                            bank = ps[:, 4 + group[0] % 4, :].rearrange("p (t n) -> p t n", n=P)
                            cols = slice(tt * P, (tt + 1) * P)
                            if kind == "cmp":
                                act.copy(xT2[0:HD, :, cols], bank[0:HD, :, :])
                                lo = 1 - tt
                                last = act.copy(xT2[HD:P, :, tt * P + lo - 1:(tt + 1) * P - 1], bank[HD:P, :, lo:P])
                            elif kind == "bq":
                                last = act.copy(bqT[:, :, cols], bank)
                            elif kind == "sw":
                                last = act.copy(swT[:, :, cols], bank[:, 0:2, :])
                            elif kind == "hid":
                                kv = tt
                                if kv == 0:
                                    act.wait_ge(hid_zeroed, layer + 1)
                                for m in (0, 1):
                                    src = ps[:, 4 + group[0] % 4, 2 * NBLK * m:2 * NBLK * (m + 1)].rearrange("p (g n) -> p g n", g=2)
                                    dst = hid[:, kv, m, 0:BKV_HEADS, 0:NBLK]
                                    if kv == 1:
                                        dst = hid[:, kv, m, :, 0:NBLK].rearrange("p (g r) n -> p g r n", g=2)
                                        src = src.unsqueeze(2).to_broadcast([P, BKV_HEADS, 4, NBLK])
                                    last = act.activation(dst, src, ACT.Gelu_apprx_tanh,
                                                          bias=ptab[:, T_B1 + 2 * kv + m:T_B1 + 2 * kv + m + 1])
                            elif kind == "cmp2":
                                act.copy(kcn[0:NBLK, 3, :], bank[0:NBLK, 0, :])
                                last = act.copy(vcn[:, :], bank[:, 1, 0:HD])
                            elif kind == "kct":
                                last = act.copy(kcT[:, 0:NBLK], bank[:, 0, 0:NBLK])
                            else:
                                last = act.copy(qkT[:, 4 * kind:4 * kind + 4, cols], bank)
                            last.then_inc(zt_evac, 1)
                            group[0] += 1

                for place, c in enumerate(Z_PLACES):
                    if c == "cmp":
                        ahead(layer, ("cmp", 1, 1))
                        used(layer, ("cmp", 1, 1))
                        act.copy(hidn[:, :, :], ps[0:2 * NBLK, 0:2, 0:CMP_HID]).then_inc(z_evac, 1)
                        turn_evac(place - 1)
                        continue
                    for half in (0, 1):
                        ahead(layer, ("z", c, half))
                    used(layer, ("z", c, 1))
                    if place in STAGING_FREE:
                        act.wait_ge(zt_turned, zt + STAGING_FREE[place])
                    pair = ps[:, 2 * (place % 2):2 * (place % 2) + 2, :]
                    st = staging[:, place % 2, :, :]
                    if c < 3:
                        last = act.copy(st, pair)
                    elif c == 3:
                        last = act.copy(va[:, :, 0:512], pair)
                    elif c == 4:
                        act.copy(va[:, :, 512:768], pair[:, :, 0:256])
                        last = act.copy(st[:, :, 0:256], pair[:, :, 256:512])
                    elif c == 5:
                        act.copy(st[:, :, 0:256], pair[:, :, 0:256])
                        for tt in range(TT):
                            src = pair[:, tt, 256:512].rearrange("p (g d) -> p g d", d=HD)
                            for twice in (0, 1):
                                last = act.copy(cmpx[:, tt, :, twice, :], src)
                    else:
                        for tt in range(TT):
                            src = pair[:, tt, :].rearrange("p (b v n) -> p b v n", b=2, v=2)
                            act.copy(st[:, tt, 0:256].rearrange("p (b n) -> p b n", b=2), src[:, :, 0, :])
                            last = act.copy(bv[:, tt, :, :], src[:, :, 1, :])
                    last.then_inc(z_evac, 1)
                    turn_evac(place - 1)
                    if place == 1:
                        act.wait_ge(prm_turned, layer + 1)
                        act.copy(ptab[:, :], ps[:, 4, 0:T_END]).then_inc(ptab_ready, 1)
                    if place == 1 and layer == 0:
                        act.wait_ge(masks_loaded, 16)
                        act.copy(cb[:, :], const_staged[:, :]).then_inc(cb_ready, 1)
                        for g in range(4):
                            hT_high(4 + g, 4 + (g + 1) % 4, memT_hi, 4 * (g % 2), g // 2)
                    if place == 2:
                        act.wait_ge(blkf_ready, 2 * (layer + 1))
                        act.copy(blk_hi[:, :, :, :], blkf[:, :, :, :]).then_inc(blk_hi_ready, 1)
                ahead(layer, ("bg",))
                used(layer, ("bg",))
                act.copy(bgn[:, :], ps[0:N_BG, 0, 0:S]).then_inc(z_evac, 1)
                turn_evac(7)
                act.wait_ge(bg_turned, layer + 1)
                act.activation(bgt[:, :, :], ps[:, 1, 0:TT * N_BG].rearrange("p (t n) -> p t n", t=TT),
                               ACT.Tanh, scale=0.5).then_inc(z_evac, 1)

                def exponentials(i):
                    kind, heads, tt = ITEMS[i]
                    c0, n, at = stat_column(i), layer * NI + i, score_at(i)
                    act.wait_ge(shift_ready, n + 1)
                    if i >= 2:
                        act.wait_ge(probT_done, n - 1)
                    wd = item_width(tt)
                    if kind == "A":
                        last = act.activation(prob[:, i % 2, 0:3 * wd], flat[:, at:at + 3 * wd], ACT.Exp, scale=SCALE,
                                              bias=stat[:, 1, c0:c0 + 1], accum_out=stat[:, 2, c0:c0 + 1])
                    elif kind == "B":
                        for r in range(item_rows(ITEMS[i])):
                            last = act.activation(prob[:, i % 2, r * wd:(r + 1) * wd], flat[:, at + r * wd:at + (r + 1) * wd],
                                                  ACT.Exp, scale=SCALE, bias=stat[:, 1, c0 + r:c0 + r + 1],
                                                  accum_out=stat[:, 2, c0 + r:c0 + r + 1])
                    else:
                        last = act.activation(prob[:, i % 2, 0:P], cs[:, :, :].rearrange("p h n -> p (h n)"), ACT.Exp, scale=SCALE)
                    last.then_inc(exp_done, 1)

                def outputs_high(g):
                    act.wait_ge(yT_done, layer * PER["yt"] + g + 1)
                    act.copy(yT_hi[:, 2 * g:2 * g + 2, :],
                             ps[:, (6, 6, 7)[g], :].rearrange("p (t n) -> p t n", t=2)).then_inc(yT_hi_ready, 1)

                def memory_out(layer, bank):
                    used(layer, ("xkv", 1))
                    act.copy(xkT[:, :, :], ps[:, bank, :].rearrange("p (t n) -> p t n", t=2))
                    act.copy(xv[:, :, :], ps[:, bank + 1, :].rearrange("p (t n) -> p t n", t=2)).then_inc(xkv_ready, 1)

                exponentials(0)
                for i in range(NI):
                    if i + 1 < NI:
                        exponentials(i + 1)
                    if i == TURN_A:
                        outputs_high(0)
                    q = gate_quarter(i)
                    if i >= FILL_WA:
                        ahead(layer, ("wa",))
                    elif q is not None:
                        if q % 2 == 0:
                            ahead(layer, ("gate", q // 4, q // 2 % 2))
                        if q % 4 == 3:
                            used(layer, ("gate", q // 4, 1))
                            act.activation(gates[:, q // 4, :, :], ps[:, 0:2, :], ACT.Tanh, scale=0.5).then_inc(z_evac, 1)

                for g in (1, 2):
                    outputs_high(g)
                ahead(layer, ("wb", 0))
                ahead(layer, ("wb", 1))
                for n in (0, 1):
                    for tt in range(TT):
                        hT_high(HT0 + layer * PER["ht"] + 2 * n + tt, 4 * n + tt, hT_hi, 4 * n, tt, scale=0.5)
                for n, half in ((0, 0), (1, 0), (0, 1)):
                    ahead(layer, ("mix", n, half))
                layer_norm_high(layer, 0, 0)
                ahead(layer, ("mix", 1, 1))

                def queries(tt):
                    n = layer * TT + tt
                    if tt == 0:
                        act.wait_ge(xq_done, layer + 1)
                    else:
                        used(layer, ("xq",))
                    act.copy(xq_n[:, tt, :], ps[:, 4 + 2 * tt, 0:S]).then_inc(xqn_ready, 1)
                    act.wait_ge(xqT_done, n + 1)
                    act.copy(xqT[:, :, tt * P:(tt + 1) * P],
                             ps[:, 5 + 2 * tt, 0:S].rearrange("p (t n) -> p t n", t=2)).then_inc(xq_ready, 1)

                def x_exponentials(x):
                    n = layer * PER["x"] + x
                    act.wait_ge(x_shift, n + 1)
                    if x >= 2:
                        act.wait_ge(x_turned, n - 1)
                    for p in (0, 1):
                        last = act.activation(xprob[:, x % 2, p * S:(p + 1) * S], ps[:, 2 * (x % 2) + p, 0:S], ACT.Exp,
                                              scale=SCALE, bias=xstat[:, 1, 2 * x + p:2 * x + p + 1],
                                              accum_out=xstat[:, 2, 2 * x + p:2 * x + p + 1])
                    last.then_inc(x_exp, 1)

                queries(0)
                if layer == 0:
                    ahead(layer, ("xkv", 0))
                    layer_norm_high(layer, 0, 1)
                    ahead(layer, ("xkv", 1))
                    memory_out(0, 0)
                    x_exponentials(0)
                    queries(1)
                    x_exponentials(1)
                    ahead(layer, ("xq",))
                else:
                    ahead(layer, ("xq",))
                    x_exponentials(0)
                    layer_norm_high(layer, 0, 1)
                    x_exponentials(1)
                    queries(1)
                x_exponentials(2)
                x_exponentials(3)
                ahead(layer, ("xo",))
                for tt in range(TT):
                    act.wait_ge(xoT_done, layer * TT + tt + 1)
                    act.copy(xoT_hi[:, :, tt * P:(tt + 1) * P],
                             ps[:, 4 * tt, 0:S].rearrange("p (t n) -> p t n", t=2)).then_inc(xoT_hi_ready, 1)
                if layer < DEPTH - 1:
                    ahead(layer + 1, ("xkv", 0))
                layer_norm_high(layer, 1, 0)
                if layer < DEPTH - 1:
                    ahead(layer + 1, ("xkv", 1))
                    memory_out(layer + 1, 6)
                layer_norm_high(layer, 1, 1)

                for it in range(FF_IT):
                    cn, fn = layer * PER["conv"] + 2 * it, layer * PER["ffn"] + it
                    for ag, name in enumerate(("ua", "ug")):
                        ahead(layer, (name, it))
                        used(layer, (name, it))
                        if ag == 0 and it >= 2:
                            act.wait_ge(hidf_ready, fn - 1)
                        for j in (0, 1):
                            t = 22 * ag + 2 * it + j
                            last = act.activation(conv_y[:, it % 2, ag, j, :], ps[:, 4 + 2 * (it % 2) + ag, j * S:(j + 1) * S],
                                                  ACT.Identity, scale=ptab[:, T_CONV + 88 + t:T_CONV + 89 + t],
                                                  bias=ptab[:, T_CB + t:T_CB + t + 1])
                        last.then_inc(conv_first, 1)
                    act.wait_ge(conv_done, cn + 1)
                    if it:
                        act.wait_ge(hidf_ready, fn)
                    act.activation(gelu_a[:, :, :], conv_y[:, it % 2, 0, :, :], ACT.Gelu_apprx_tanh).then_inc(gelu_done, 1)
                    if it:
                        ahead(layer, ("down", it - 1))
                    act.wait_ge(hidf_ready, fn + 1)
                    if it >= 2:
                        used(layer, ("down", it - 2))
                    act.copy(hid_hi[:, it % 2, :, :], hidf[:, :, :]).then_inc(hid_hi_ready, 1)
                ahead(layer, ("down", FF_IT - 1))
                if layer < DEPTH - 1:
                    layer_norm_high(layer, 2, 0)
                    ahead(layer + 1, ("z", Z_PLACES[0], 0))
                    layer_norm_high(layer, 2, 1)

        @block.vector
        def _(dve):
            done = [0]
            steps = [0]
            rope_count = [0]

            def step(ins):
                steps[0] += 1
                ins.then_inc(dve_step, 1)

            def settle():
                dve.wait_ge(dve_step, steps[0])

            def split_through(n):
                while done[0] <= n and done[0] < NU:
                    k = done[0]
                    dve.wait_ge(hi_split, k + 1)
                    size = KT * N_BG if UNITS[k][1] == ("bg",) else UNIT
                    dve.tensor_tensor(w_lo[:, k % SPLIT, 0:size], raw[:, k % RAW, 0:size],
                                      w_hi[:, k % SPLIT, 0:size].bitcast(F32), ALU.subtract).then_inc(lo_split, 1)
                    done[0] += 1

            def ahead(layer, name):
                split_through(UNIT_AT[layer, name] + SPLIT - 1)

            def hT_low(group, bank, hi, lo, tile0, tt, scale=None):
                cols = slice(tt * P, (tt + 1) * P)
                high = hi[:, tile0:tile0 + 4, cols].bitcast(F32)
                src = ps[:, bank, :].rearrange("p (t n) -> p t n", n=P)
                dve.wait_ge(hT_hi_ready, group + 1)
                if scale is None:
                    last = dve.tensor_tensor(lo[:, tile0:tile0 + 4, cols], src, high, ALU.subtract)
                else:
                    last = dve.scalar_tensor_tensor(out=lo[:, tile0:tile0 + 4, cols], in0=src, scalar=scale, in1=high,
                                                    op0=ALU.mult, op1=ALU.subtract)
                last.then_inc(hT_lo_ready, 1)

            def layer_norm(layer, k, tt, last_unit, between=None):
                if tt == 0:
                    dve.wait_ge(res_done, 3 * layer + k + 1)
                else:
                    dve.wait_ge(unit_used, UNIT_AT[layer, last_unit] + 1)
                for c in (0, 1):
                    cols = slice(512 * c, 512 * (c + 1))
                    step(dve.scalar_tensor_tensor(out=h[:, tt, cols], in0=h[:, tt, cols], scalar=ALPHA,
                                                  in1=ps[:, 2 * tt + c, :], op0=ALU.mult, op1=ALU.add))
                summed = steps[0]
                if between:
                    between()
                for c in (0, 1):
                    dve.wait_ge(dve_step, summed - 1 + c)
                    step(dve.bn_stats(lnst[:, tt, c, :], h[:, tt, 512 * c:512 * (c + 1)]))
                settle()
                step(dve.bn_aggr(lnmv[:, tt, :], lnst[:, tt, :, :].rearrange("p a b -> p (a b)")))
                settle()
                dve.wait_ge(gb_loaded, 32 * (3 * layer + k + 1))
                v, r, a, b = (lnv[:, tt, i:i + 1] for i in range(4))

                def link(e):
                    if e == 0:
                        return dve.tensor_scalar(a.bitcast(I32), v.bitcast(I32), 1, None, ALU.logical_shift_right)
                    if e == 1:
                        return dve.tensor_scalar(r.bitcast(I32), a.bitcast(I32), -1.0, float(0x5F3759DF), ALU.mult, ALU.add)
                    if e % 2 == 0:
                        return dve.scalar_tensor_tensor(out=a, in0=r, scalar=b, in1=r, op0=ALU.mult, op1=ALU.mult)
                    return dve.scalar_tensor_tensor(out=r, in0=a, scalar=1.5, in1=r, op0=ALU.add, op1=ALU.mult)

                step(dve.tensor_scalar(b, lnmv[:, tt, 1:2], LN_EPS, -0.5, ALU.add, ALU.mult))
                step(dve.tensor_scalar(v, lnmv[:, tt, 1:2], LN_EPS, None, ALU.add))
                for e in range(8):
                    before = steps[0]
                    cols = slice(P * e, P * (e + 1))
                    step(dve.scalar_tensor_tensor(out=h[:, tt, cols], in0=h[:, tt, cols], scalar=lnmv[:, tt, 0:1],
                                                  in1=gb[:, 0, cols], op0=ALU.subtract, op1=ALU.mult))
                    dve.wait_ge(dve_step, before)
                    step(link(e))
                settle()
                for c in (0, 1):
                    cols = slice(512 * c, 512 * (c + 1))
                    dve.scalar_tensor_tensor(out=h[:, tt, cols], in0=h[:, tt, cols], scalar=r,
                                             in1=gb[:, 1, cols], op0=ALU.mult, op1=ALU.add).then_inc(ln_done, 1)

            def layer_norm_low(layer, k, tt):
                for half in (0, 1):
                    hT_low(HT0 + layer * PER["ht"] + 4 * (k + 1) + 2 * tt + half, turned_bank(k, tt) + half, hT_hi, hT_lo, 4 * half, tt)

            for g in range(4):
                if g == 2:
                    split_through(SPLIT - 1)
                hT_low(g, 4 + g, hT_hi, hT_lo, 4 * (g % 2), g // 2)
            dve.wait_ge(const_loaded, 16)

            for layer in range(DEPTH):
                base = layer * PER["z_evac"]
                zt = layer * PER["zt"]

                def rope(place, n_heads):
                    dve.wait_ge(z_evac, base + place + 1)
                    if rope_count[0]:
                        dve.wait_ge(roped, rope_count[0])
                    rope_count[0] += 1
                    n = HD * n_heads
                    heads = lambda t: t.rearrange("p t (g d) -> p t g d", d=HD)
                    x = heads(staging[:, place % 2, :, 0:n])
                    ta, tb = heads(rope_a[:, :, 0:n]), heads(rope_b[:, :, 0:n])
                    table = lambda at: cf[:, at:at + TT * HD].rearrange("p (t d) -> p t d", t=TT)
                    cos = table(F_COS).unsqueeze(2).to_broadcast([P, TT, n_heads, HD])
                    sin = table(F_SIN).unsqueeze(2).to_broadcast([P, TT, n_heads, HD])
                    step(dve.tensor_tensor(ta, x, cos, ALU.mult))
                    half = HD // 2
                    step(dve.tensor_tensor(tb[:, :, :, 0:half], x[:, :, :, half:HD], sin[:, :, :, 0:half], ALU.mult))
                    step(dve.tensor_tensor(tb[:, :, :, half:HD], x[:, :, :, 0:half], sin[:, :, :, half:HD], ALU.mult))
                    settle()
                    if place < 2:
                        for tt in range(TT):
                            pairs = staging[:, 0, tt, :].rearrange("p (j a d) -> p j a d", a=2, d=HD)
                            last = dve.tensor_tensor(pairs[:, :, place, :], ta[:, tt], tb[:, tt], ALU.add)
                            if tt == 0:
                                step(last)
                    else:
                        last = dve.tensor_tensor(x, ta, tb, ALU.add)
                    last.then_inc(roped, 1)

                for place, c in enumerate(Z_PLACES):
                    if c == "cmp":
                        ahead(layer, ("cmp", 1, 1))
                        continue
                    for half in (0, 1):
                        ahead(layer, ("z", c, half))
                    if place == 2:
                        dve.wait_ge(ptab_ready, layer + 1)
                        dve.wait_ge(zt_evac, zt + groups_until("cmp"))
                        for kv in (0, 1):
                            for g in range(BKV_HEADS):
                                src = xT2[:, 2 * kv + g, :].rearrange("p (n j a) -> p j n a", a=2, j=8)
                                for up in (0, 1):
                                    pos = ptab[:, T_POS + 16 * kv + 8 * up:T_POS + 16 * kv + 8 * (up + 1)]
                                    last = dve.tensor_tensor(
                                        blkf[:, kv, 8 * up:8 * (up + 1), NBLK * g:NBLK * (g + 1)],
                                        src[:, :, up:up + NBLK, 0],
                                        pos.unsqueeze(2).to_broadcast([P, 8, NBLK]), ALU.add)
                            last.then_inc(blkf_ready, 1)
                    if c != 3:
                        rope(place, 8 if c < 3 else 4)
                    if place == 1 and layer == 0:
                        for g in range(4):
                            hT_low(4 + g, 4 + (g + 1) % 4, memT_hi, memT_lo, 4 * (g % 2), g // 2)
                    if place == 2:
                        dve.wait_ge(blk_hi_ready, layer + 1)
                        dve.tensor_tensor(blk_lo[:, :, :, :].rearrange("p v j n -> p (v j n)"),
                                          blkf[:, :, :, :].rearrange("p v j n -> p (v j n)"),
                                          blk_hi[:, :, :, :].rearrange("p v j n -> p (v j n)").bitcast(F32),
                                          ALU.subtract).then_inc(blk_lo_ready, 1)
                    if place == 6:
                        dve.wait_ge(zt_evac, zt + groups_until("cmp2"))
                        k0, k1, k2, kc = (kcn[0:NBLK, m, :].rearrange("p (g d) -> p g d", d=HD) for m in range(4))
                        cos = cf[0:NBLK, F_KC:F_KC + HD].unsqueeze(1).to_broadcast([NBLK, BKV_HEADS, HD])
                        sin = cf[0:NBLK, F_KS:F_KS + HD].unsqueeze(1).to_broadcast([NBLK, BKV_HEADS, HD])
                        half = HD // 2
                        step(dve.tensor_tensor(k1, kc, cos, ALU.mult))
                        step(dve.tensor_tensor(k2[:, :, 0:half], kc[:, :, half:HD], sin[:, :, 0:half], ALU.mult))
                        step(dve.tensor_tensor(k2[:, :, half:HD], kc[:, :, 0:half], sin[:, :, half:HD], ALU.mult))
                        settle()
                        dve.tensor_tensor(k0, k1, k2, ALU.add).then_inc(cmp_vec, 1)
                        dve.tensor_tensor(vcbd[:, :, :], vcn[:, :].unsqueeze(1).to_broadcast([P, BQ_HEADS, HD]),
                                          cf[:, F_BD:F_BD + BQ_HEADS].unsqueeze(2).to_broadcast([P, BQ_HEADS, HD]),
                                          ALU.mult).then_inc(cmp_vec, 1)
                ahead(layer, ("bg",))
                dve.wait_ge(z_evac, base + BG_EVAC)
                step(dve.tensor_scalar(bgt[:, :, :], bgt[:, :, :], 1.0, 0.5, ALU.add, ALU.mult))

                def out_evac(i):
                    kind, heads, tt = ITEMS[i]
                    c0 = stat_column(i)
                    dve.wait_ge(pv_done, layer * NI + i + 1)
                    if kind == "A":
                        last = dve.tensor_scalar(y[:, tt, HD * heads:HD * (heads + 1)], flat[:, OUT:OUT + HD],
                                                 stat[:, 3, c0:c0 + 1], None, ALU.mult)
                    elif kind == "C":
                        last = dve.tensor_tensor(
                            y[:, tt, 256:768].rearrange("p (g d) -> p g d", d=HD),
                            ps[:, 7, :].rearrange("p (g d) -> p g d", d=HD),
                            coef[:, c0:c0 + BQ_HEADS].unsqueeze(2).to_broadcast([P, BQ_HEADS, HD]), ALU.mult)
                    else:
                        dve.wait_ge(o_evac, layer * NI + i)
                        for br in (0, 1):
                            for a, hd in enumerate(heads):
                                r = 2 * a + br
                                yh = y[:, tt, 256 + HD * hd:256 + HD * (hd + 1)]
                                last = dve.scalar_tensor_tensor(out=yh, in0=flat[:, OUT + HD * r:OUT + HD * (r + 1)],
                                                                scalar=coef[:, c0 + r:c0 + r + 1], in1=yh,
                                                                op0=ALU.mult, op1=ALU.add)
                                if br == 0:
                                    step(last)
                            if br == 0:
                                settle()
                    last.then_inc(o_evac, 1)

                def maximum(i):
                    kind, heads, tt = item = ITEMS[i]
                    rows, wd, c0, n, at = item_rows(item), item_width(tt), stat_column(i), layer * NI + i, score_at(i)
                    mx, shift = stat[:, 0, c0:c0 + rows], stat[:, 1, c0:c0 + rows]
                    dve.wait_ge(scores_done, n + 1)
                    if kind == "A":
                        step(dve.reduce_max(mx, flat[:, at:at + 3 * wd], AX.X))
                    elif kind == "B":
                        step(dve.reduce_max(mx, flat[:, at:at + rows * wd].rearrange("p (r n) -> p r n", r=rows), AX.X))
                    else:
                        compressed = flat[:, at:at + 1024].rearrange("p (v m) -> p v m", v=2)[:, :, 0:64].rearrange(
                            "p v (r n) -> p v r n", n=16)
                        step(dve.tensor_reduce(mx.rearrange("p (v r) -> p v r", v=2), compressed, AX.X, ALU.max))
                    settle()
                    if kind == "C":
                        step(dve.tensor_scalar(shift, mx, FLOOR, None, ALU.max))
                        settle()
                        dve.wait_ge(exp_done, n)
                        dve.tensor_tensor(cs[:, :, :].rearrange("p (v r) n -> p v r n", v=2), compressed,
                                          shift.unsqueeze(2).to_broadcast([P, rows, 16]).rearrange("p (v r) n -> p v r n", v=2),
                                          ALU.subtract).then_inc(shift_ready, 1)
                    else:
                        dve.tensor_scalar(shift, mx, -SCALE, None, ALU.mult).then_inc(shift_ready, 1)

                def outputs_low(g):
                    dve.wait_ge(yT_hi_ready, layer * PER["yt"] + g + 1)
                    dve.tensor_tensor(yT_lo[:, 2 * g:2 * g + 2, :], ps[:, (6, 6, 7)[g], :].rearrange("p (t n) -> p t n", t=2),
                                      yT_hi[:, 2 * g:2 * g + 2, :].bitcast(F32), ALU.subtract).then_inc(yT_lo_ready, 1)

                def gate_a(n):
                    dve.scalar_tensor_tensor(out=gates[:, n, :, :], in0=gates[:, n, :, :], scalar=1.0,
                                             in1=ps[:, 2 * n:2 * n + 2, :], op0=ALU.add, op1=ALU.mult).then_inc(a_gated, 1)

                maximum(0)
                for i, item in enumerate(ITEMS):
                    kind, heads, tt = item
                    rows, c0, n = item_rows(item), stat_column(i), layer * NI + i
                    if i + 1 < NI:
                        maximum(i + 1)
                    if i == TURN_A:
                        outputs_low(0)
                    if i == NI - 1:
                        ahead(layer, ("wa",))
                    q = gate_quarter(i)
                    if i % 2 and q is not None:
                        ahead(layer, ("gate", q // 4, q // 2 % 2))
                    if i:
                        settle()
                        out_evac(i - 1)
                    dve.wait_ge(exp_done, n + 1)
                    lsum, rsum = stat[:, 2, c0:c0 + rows], stat[:, 3, c0:c0 + rows]
                    if kind == "C":
                        step(dve.reduce_sum(lsum, prob[:, i % 2, 0:P].rearrange("p (r n) -> p r n", r=rows), AX.X))
                        settle()
                        step(dve.tensor_scalar(lsum, lsum, 1e-30, None, ALU.max))
                        settle()
                    step(dve.reciprocal(rsum, lsum))
                    if kind != "A":
                        settle()
                        gate = bgt[:, tt, :].rearrange("p (g b) -> p g b", b=3)
                        if kind == "C":
                            step(dve.tensor_tensor(coef[:, c0:c0 + rows], rsum, gate[:, :, 0], ALU.mult))
                        else:
                            h0, nh = heads[0], len(heads)
                            step(dve.tensor_tensor(coef[:, c0:c0 + rows].rearrange("p (g b) -> p g b", b=2),
                                                   rsum.rearrange("p (g b) -> p g b", b=2), gate[:, h0:h0 + nh, 1:3], ALU.mult))
                    nb = item_blocks(item)
                    dve.wait_ge(probT_done, n + 1)
                    if i >= 2:
                        dve.wait_ge(pv_done, n - 1)
                    dve.tensor_copy(probT[:, i % 2, 0:P * nb], flat[:, TURNED:TURNED + P * nb]).then_inc(probT_evac, 1)
                settle()
                out_evac(NI - 1)

                for g in (1, 2):
                    outputs_low(g)
                dve.wait_ge(wa_done, layer + 1)
                gate_a(0)
                dve.wait_ge(unit_used, UNIT_AT[layer, ("wa",)] + 1)
                gate_a(1)
                for n in (0, 1):
                    ahead(layer, ("wb", n))
                    dve.wait_ge(unit_used, UNIT_AT[layer, ("wb", n)] + 1)
                    step(dve.scalar_tensor_tensor(out=gates[:, 2 + n, :, :], in0=gates[:, 2 + n, :, :], scalar=1.0,
                                                  in1=ps[:, 4 + 2 * n:6 + 2 * n, :], op0=ALU.add, op1=ALU.mult))
                    settle()
                    dve.wait_ge(a_gated, 2 * (layer + 1))
                    dve.tensor_tensor(gates[:, n, :, :], gates[:, n, :, :], gates[:, 2 + n, :, :], ALU.add).then_inc(merged, 1)
                    for tt in range(TT):
                        hT_low(HT0 + layer * PER["ht"] + 2 * n + tt, 4 * n + tt, hT_hi, hT_lo, 4 * n, tt, scale=0.5)
                ahead(layer, ("mix", 0, 0))
                ahead(layer, ("mix", 1, 0))
                layer_norm(layer, 0, 0, None)
                layer_norm_low(layer, 0, 0)
                ahead(layer, ("mix", 0, 1))
                if layer == 0:
                    ahead(layer, ("mix", 1, 1))
                layer_norm(layer, 0, 1, ("mix", 1, 1))

                def x_maximum(x):
                    mx, shift = xstat[:, 0, 2 * x:2 * x + 2], xstat[:, 1, 2 * x:2 * x + 2]
                    dve.wait_ge(x_scores, layer * PER["x"] + x + 1)
                    step(dve.reduce_max(mx, ps[:, 2 * (x % 2):2 * (x % 2) + 2, 0:S], AX.X))
                    settle()
                    dve.tensor_scalar(shift, mx, -SCALE, None, ALU.mult).then_inc(x_shift, 1)

                def x_probabilities(x):
                    n = layer * PER["x"] + x
                    dve.wait_ge(x_exp, n + 1)
                    step(dve.reciprocal(xstat[:, 3, 2 * x:2 * x + 2], xstat[:, 2, 2 * x:2 * x + 2]))
                    dve.wait_ge(x_turned, n + 1)
                    if x >= 2:
                        dve.wait_ge(x_pv, n - 1)
                    else:
                        dve.wait_ge(pv_done, NI * (layer + 1))
                    dve.tensor_copy(probT[:, x % 2, 0:512], ps[:, 4 + x % 2, :]).then_inc(x_probT, 1)

                def x_outputs(x):
                    tt, j = x // 2, x % 2
                    settle()
                    dve.wait_ge(x_pv, layer * PER["x"] + x + 1)
                    dve.tensor_tensor(xo_n[:, tt, P * j:P * (j + 1)].rearrange("p (g d) -> p g d", d=HD),
                                      ps[:, 6 + x % 2, 0:P].rearrange("p (g d) -> p g d", d=HD),
                                      xstat[:, 3, 2 * x:2 * x + 2].unsqueeze(2).to_broadcast([P, 2, HD]),
                                      ALU.mult).then_inc(x_evac, 1)

                def xo_low(tt):
                    dve.wait_ge(xoT_hi_ready, layer * TT + tt + 1)
                    cols = slice(tt * P, (tt + 1) * P)
                    dve.tensor_tensor(xoT_lo[:, :, cols], ps[:, 4 * tt, 0:S].rearrange("p (t n) -> p t n", t=2),
                                      xoT_hi[:, :, cols].bitcast(F32), ALU.subtract).then_inc(xoT_lo_ready, 1)

                if layer == 0:
                    layer_norm_low(layer, 0, 1)
                    ahead(layer, ("xkv", 0))
                    x_maximum(0)
                else:
                    x_maximum(0)
                    layer_norm_low(layer, 0, 1)
                x_maximum(1)
                x_probabilities(0)
                ahead(layer, ("xkv", 1) if layer == 0 else ("mix", 1, 1))
                x_maximum(2)
                x_probabilities(1)
                x_outputs(0)
                x_maximum(3)
                if layer < DEPTH - 1:
                    ahead(layer, ("xq",))
                x_probabilities(2)
                x_outputs(1)
                x_probabilities(3)
                x_outputs(2)
                xo_low(0)
                x_outputs(3)
                xo_low(1)
                ahead(layer, ("xo",) if layer < DEPTH - 1 else ("xq",))
                layer_norm(layer, 1, 0, None)
                layer_norm(layer, 1, 1, ("xo",))
                for tt in range(TT):
                    layer_norm_low(layer, 1, tt)
                if layer < DEPTH - 1:
                    ahead(layer + 1, ("xkv", 0))
                    ahead(layer + 1, ("xkv", 1))
                else:
                    ahead(layer, ("xo",))

                for it in range(FF_IT):
                    cn, fn = layer * PER["conv"] + 2 * it, layer * PER["ffn"] + it
                    for ag, name in enumerate(("ua", "ug")):
                        ahead(layer, (name, it))
                        dve.wait_ge(conv_first, cn + ag + 1)
                        for back in (1, 2):
                            for j in (0, 1):
                                t = 22 * ag + 2 * it + j
                                tap = ptab[:, T_CONV + 44 * (2 - back) + t:T_CONV + 44 * (2 - back) + t + 1]
                                acc = conv_y[:, it % 2, ag, j, back:S]
                                last = dve.scalar_tensor_tensor(
                                    out=acc, in0=ps[:, 4 + 2 * (it % 2) + ag, j * S:(j + 1) * S - back],
                                    scalar=tap, in1=acc, op0=ALU.mult, op1=ALU.add)
                                if back == 1:
                                    step(last)
                            if back == 1:
                                settle()
                        last.then_inc(conv_done, 1)
                    dve.wait_ge(gelu_done, fn + 1)
                    dve.wait_ge(conv_done, cn + 2)
                    dve.tensor_tensor(hidf[:, :, :], gelu_a[:, :, :], conv_y[:, it % 2, 1, :, :], ALU.mult).then_inc(hidf_ready, 1)
                    if it:
                        ahead(layer, ("down", it - 1))
                    dve.wait_ge(hid_hi_ready, fn + 1)
                    dve.wait_ge(hidf_ready, fn + 1)
                    dve.tensor_tensor(hid_lo[:, it % 2, :, :], hidf[:, :, :], hid_hi[:, it % 2, :, :].bitcast(F32),
                                      ALU.subtract).then_inc(hid_lo_ready, 1)
                ahead(layer, ("down", FF_IT - 1))
                more = layer < DEPTH - 1
                layer_norm(layer, 2, 0, None)
                layer_norm(layer, 2, 1, ("down", FF_IT - 1), (lambda: layer_norm_low(layer, 2, 0)) if more else None)
                if more:
                    ahead(layer + 1, ("z", Z_PLACES[0], 0))
                    layer_norm_low(layer, 2, 1)

        @block.tensor
        def _(pe):
            def product(dst, s_hi, s_lo, m_hi, m_lo, start, stop):
                pe.matmul(dst, s_hi, m_hi, start=start, stop=False, skip_group_check=True)
                pe.matmul(dst, s_hi, m_lo, start=False, stop=False, skip_group_check=True)
                return pe.matmul(dst, s_lo, m_hi, start=False, stop=stop, skip_group_check=True)

            def take(layer, name):
                n = UNIT_AT[layer, name]
                pe.wait_ge(lo_split, n + 1)
                return unit_view(w_hi, n % SPLIT, name), unit_view(w_lo, n % SPLIT, name)

            def turn(group_sem, bank, sources):
                for b, src in enumerate(sources):
                    last = pe.transpose(ps[:, bank, b * P:(b + 1) * P], src, ident)
                last.then_inc(group_sem, 1)

            def turn_h(tt, half, bank):
                turn(hT_turned, bank, [h[:, tt, 512 * half + P * b:512 * half + P * (b + 1)] for b in range(4)])

            def keep_warm(bank, n):
                for _ in range(n):
                    pe.matmul(ps[:, bank, :], identb, cb[:, 0:512], start=True, stop=True, skip_group_check=True)

            def layer_norm_turn(layer, k, tt):
                for half in (0, 1):
                    pe.wait_ge(ln_done, layer * PER["ln"] + 4 * k + 2 * tt + half + 1)
                    turn_h(tt, half, turned_bank(k, tt) + half)

            def columns(layer, name, halves, bank0, width, k_of, k_stop, tiles=range(TT)):
                whi, wlo = take(layer, name)
                for kk in halves:
                    k = k_of + kk
                    for tt in tiles:
                        cols = slice(tt * P, (tt + 1) * P)
                        last = product(ps[:, bank0 + tt, 0:width], hT_hi[:, k, cols], hT_lo[:, k, cols],
                                       whi[:, kk, :], wlo[:, kk, :], k == 0, k == k_stop)
                return last

            def memory_product(layer, half, tiles, bank):
                whi, wlo = take(layer, ("xkv", half))
                for kk in tiles:
                    k = 4 * half + kk
                    for j in (0, 1):
                        cols = slice(j * P, (j + 1) * P)
                        product(ps[:, bank, S * j:S * (j + 1)], whi[:, kk, cols], wlo[:, kk, cols],
                                memT_hi[:, k, :], memT_lo[:, k, :], k == 0 and j == 0, k == 7)
                    for j in (0, 1):
                        cols = slice(j * P, (j + 1) * P)
                        last = product(ps[:, bank + 1, S * j:S * (j + 1)], memT_hi[:, k, cols], memT_lo[:, k, cols],
                                       whi[:, kk, S:2 * S], wlo[:, kk, S:2 * S], k == 0 and j == 0, k == 7)
                return last

            def input_turn(layer, tt):
                if layer:
                    layer_norm_turn(layer - 1, 2, tt)
                else:
                    pe.wait_ge(x_loaded[tt], 16)
                    for half in (0, 1):
                        turn_h(tt, half, 4 + 2 * tt + half)

            pe.wait_ge(const_loaded, 16)
            for layer in range(DEPTH):
                base = layer * PER["z_evac"]
                zt = layer * PER["zt"]
                ht = HT0 + layer * PER["ht"]

                input_turn(layer, 0)
                if layer == 0:
                    for _ in range(3):
                        pe.matmul(ps[:, 0, :], ident, cf[:, 0:512], start=True, stop=True, skip_group_check=True)
                pe.wait_ge(hT_lo_ready, start_group(layer) + 2)
                group = [0]

                def compression_turn(kind, kv, bank):
                    if kind == "hid":
                        pe.wait_ge(z_evac, base + Z_PLACES.index("cmp") + 1)
                        for m in (0, 1):
                            last = pe.transpose(ps[:, bank, 2 * NBLK * m:2 * NBLK * (m + 1)], hidn[:, kv, P * m:P * (m + 1)],
                                                ident[0:2 * NBLK, 0:2 * NBLK])
                    elif kind == "cmp2":
                        pe.wait_ge(zt_evac, zt + groups_until("hid"))
                        for g in range(BKV_HEADS):
                            for m in (0, 1):
                                pe.matmul(ps[0:NBLK, bank, HD * g:HD * (g + 1)], hid[:, 0, m, g, 0:NBLK], w2[:, 0, m, :],
                                          start=(m == 0), stop=(m == 1), skip_group_check=True)
                        for m in (0, 1):
                            rep = hid[:, 1, m, :, :].rearrange("p h n -> p (h n)")
                            last = pe.matmul(ps[:, bank, P:P + HD], rep, w2[:, 1, m, :], start=(m == 0), stop=(m == 1),
                                             skip_group_check=True)
                    else:
                        pe.wait_ge(cmp_vec, 2 * layer + 2)
                        last = pe.transpose(ps[:, bank, 0:NBLK], kcn[0:NBLK, 0, :], ident[0:NBLK, 0:NBLK])
                    last.then_inc(zt_turned, 1)

                def z_turn(place):
                    for kind in Z_GROUPS.get(place, ()):
                        for tt in range(TT if kind in TWO else 1):
                            bank = 4 + group[0] % 4
                            if group[0] == 0:
                                pe.wait_ge(ptab_ready, layer + 1)
                                if layer == 0:
                                    pe.wait_ge(hT_lo_ready, HT0)
                                pe.wait_ge(z_evac, base + 2)
                            if kind in ROPES_BEFORE:
                                pe.wait_ge(roped, layer * PER["roped"] + ROPES_BEFORE[kind])
                            if group[0] >= 4:
                                pe.wait_ge(zt_evac, zt + group[0] - 3)
                            if kind in ("hid", "cmp2", "kct"):
                                compression_turn(kind, tt, bank)
                                group[0] += 1
                                continue
                            if kind == "cmp":
                                src = [cmpx[:, tt, b, :, :].rearrange("p a d -> p (a d)") for b in range(4)]
                            elif kind == "bq":
                                src = [staging[:, 0, tt, P * b:P * (b + 1)] for b in range(4)]
                            elif kind == "sw":
                                src = [staging[:, place % 2, tt, P * b:P * (b + 1)] for b in range(2)]
                            else:
                                src = [staging[:, place % 2, tt, P * b:P * (b + 1)] for b in range(4)]
                            turn(zt_turned, 4 + group[0] % 4, src)
                            group[0] += 1

                for tt in range(TT):
                    for place, c in enumerate(Z_PLACES[:2]):
                        for half in (0, 1):
                            last = columns(layer, ("z", c, half), range(4), 2 * place, 512, 4 * half, 7, (tt,))
                            if tt:
                                last.then_inc(unit_used, 1)
                        if tt == 0 and place == 0:
                            input_turn(layer, 1)
                    if tt == 0:
                        pe.wait_ge(hT_lo_ready, start_group(layer) + 4)
                pe.wait_ge(prm_loaded, 80 * (layer + 1))
                for b in range(4):
                    pe.transpose(ps[:, 4, 44 * b:44 * (b + 1)], prm_c[:, b, :], ident[0:44, 0:44])
                for b in (0, 1):
                    pe.transpose(ps[:, 4, T_POS + 16 * b:T_POS + 16 * (b + 1)], prm_p[:, b, :], ident[0:16, 0:16])
                pe.transpose(ps[:, 4, T_B1:T_B1 + 4], prm_b[:, :], ident[0:4, 0:4]).then_inc(prm_turned, 1)
                if layer == 0:
                    pe.wait_ge(mem_loaded, 16)
                    for g in range(4):
                        if g == 3:
                            pe.wait_ge(ptab_ready, 1)
                        turn(hT_turned, 4 + (g + 1) % 4,
                             [mem_n[:, g // 2, 512 * (g % 2) + P * b:512 * (g % 2) + P * (b + 1)] for b in range(4)])
                for place, c in enumerate(Z_PLACES):
                    if place < 2:
                        continue
                    pe.wait_ge(z_evac, base + place - 1)
                    if c == "cmp":
                        pe.wait_ge(blk_lo_ready, layer + 1)
                        for kv in (0, 1):
                            for half in (0, 1):
                                whi, wlo = take(layer, ("cmp", kv, half))
                                for kk in range(8):
                                    k = 8 * half + kk
                                    last = product(ps[0:2 * NBLK, kv, 0:CMP_HID], blk_hi[:, kv, k, :], blk_lo[:, kv, k, :],
                                                   whi[:, kk, :], wlo[:, kk, :], k == 0, k == 15)
                                last.then_inc(unit_used, 1)
                        z_turn(place - 1)
                        continue
                    for half in (0, 1):
                        columns(layer, ("z", c, half), range(4), 2 * (place % 2), 512, 4 * half, 7).then_inc(unit_used, 1)
                    z_turn(place - 1)
                pe.wait_ge(z_evac, base + len(Z_PLACES) - 1)
                whi, wlo = take(layer, ("bg",))
                for k in range(KT):
                    last = product(ps[0:N_BG, 0, 0:S], whi[:, k, :], wlo[:, k, :], hT_hi[:, k, :], hT_lo[:, k, :],
                                   k == 0, k == KT - 1)
                last.then_inc(unit_used, 1)
                z_turn(7)
                pe.wait_ge(z_evac, base + BG_EVAC - 1)
                for tt in range(TT):
                    last = pe.transpose(ps[:, 1, N_BG * tt:N_BG * (tt + 1)], bgn[:, tt * P:(tt + 1) * P],
                                        ident[0:N_BG, 0:N_BG])
                last.then_inc(bg_turned, 1)

                def scores(i):
                    kind, heads, tt = ITEMS[i]
                    wd, at = item_width(tt), score_at(i)
                    q = slice(tt * P, (tt + 1) * P)
                    if i == 0:
                        pe.wait_ge(cb_ready, 1)
                        pe.wait_ge(z_evac, base + len(Z_PLACES))
                        pe.wait_ge(zt_evac, zt + Z_T)
                    elif i >= 2:
                        pe.wait_ge(exp_done, layer * NI + i - 1)
                    if kind == "A":
                        mask = B_A0 if tt == 0 else B_A1
                        for c in range(0, 3 * wd, 512):
                            n = min(512, 3 * wd - c)
                            pe.matmul(flat[:, at + c:at + c + n], identb, cb[:, mask + c:mask + c + n],
                                      start=True, stop=False, skip_group_check=True)
                        for g in range(A_GROUPS):
                            head = A_HPG * g + heads
                            part = slice(HD * (head % 2), HD * (head % 2) + HD)
                            last = pe.matmul(flat[:, at + g * wd:at + (g + 1) * wd], qkT[part, head // 2, q],
                                             qkT[part, 6 + head // 2, 0:wd], start=False, stop=True, skip_group_check=True)
                    elif kind == "B":
                        mask = B_B0 if tt == 0 else B_B1
                        rows = item_rows(ITEMS[i])
                        pe.matmul(flat[:, at:at + rows * wd], identb,
                                  cb[:, mask:mask + wd].unsqueeze(1).to_broadcast([P, rows, wd]),
                                  start=True, stop=False, skip_group_check=True)
                        for a, hd in enumerate(heads):
                            kv = hd // 4
                            part = slice(HD * kv, HD * kv + HD)
                            for br in (0, 1):
                                r = 2 * a + br
                                last = pe.matmul(flat[:, at + r * wd:at + (r + 1) * wd], bqT[part, hd % 4, q],
                                                 swT[part, br, 0:wd], start=False, stop=True, skip_group_check=True)
                    else:
                        mask = B_C + 16 * tt
                        for kv in range(BKV_HEADS):
                            pe.matmul(ps[:, at // 512 + kv, 0:64], identb,
                                      cb[:, mask:mask + 16].unsqueeze(1).to_broadcast([P, 4, 16]),
                                      start=True, stop=False, skip_group_check=True)
                        for hd in range(BQ_HEADS):
                            part = slice(HD * (hd // 4), HD * (hd // 4) + HD)
                            last = pe.matmul(ps[:, at // 512 + hd // 4, 16 * (hd % 4):16 * (hd % 4) + NBLK], bqT[part, hd % 4, q],
                                             kcT[part, 0:NBLK], start=False, stop=True, skip_group_check=True)
                    last.then_inc(scores_done, 1)

                def outputs_turn_y(g):
                    turn(yT_done, (6, 6, 7)[g], [y[:, tt, P * (2 * g + t):P * (2 * g + t + 1)] for t in (0, 1) for tt in range(TT)])

                def branch(name, tile0, n_tiles, col, bank0, tiles=range(4), token_tiles=range(TT)):
                    whi, wlo = take(layer, name)
                    for k in tiles[:n_tiles]:
                        for tt in token_tiles:
                            cols = slice(tt * P, (tt + 1) * P)
                            last = product(ps[:, bank0 + tt, :], yT_hi[:, tile0 + k, cols], yT_lo[:, tile0 + k, cols],
                                           whi[:, k, col:col + 512], wlo[:, k, col:col + 512], k == 0, k == n_tiles - 1)
                    return last

                def filler(i):
                    if i == 0:
                        pe.wait_ge(z_evac, base + BG_EVAC)
                    if i == TURN_A:
                        outputs_turn_y(0)
                    q = gate_quarter(i)
                    if i == FILL_WA:
                        pe.wait_ge(z_evac, base + PER["z_evac"])
                        branch(("wa",), 0, 2, 0, 0, (0,))
                    elif q is not None:
                        c, half = q // 4, q // 2 % 2
                        if q and q % 4 == 0:
                            pe.wait_ge(z_evac, base + BG_EVAC + c)
                        two = range(2 * (q % 2), 2 * (q % 2) + 2)
                        last = columns(layer, ("gate", c, half), two, 0, 512, 4 * half, 7)
                        if q % 2:
                            last.then_inc(unit_used, 1)

                def prob_turn(i):
                    pe.wait_ge(exp_done, layer * NI + i + 1)
                    if i == TURN_A:
                        pe.wait_ge(yT_lo_ready, layer * PER["yt"] + 1)
                    if i:
                        pe.wait_ge(probT_evac, layer * NI + i)
                    for b in range(item_blocks(ITEMS[i])):
                        if b == 4:
                            pe.wait_ge(o_evac, layer * NI + i)
                        last = pe.transpose(flat[:, TURNED + P * b:TURNED + P * (b + 1)], prob[:, i % 2, P * b:P * (b + 1)], ident)
                    last.then_inc(probT_done, 1)

                def values(i):
                    kind, heads, tt = ITEMS[i]
                    pe.wait_ge(probT_evac, layer * NI + i + 1)
                    if i:
                        pe.wait_ge(o_evac, layer * NI + i)
                    blocks = tt + 1
                    if kind == "A":
                        for g in range(A_GROUPS):
                            head = A_HPG * g + heads
                            for kt in range(blocks):
                                b = g * blocks + kt
                                last = pe.matmul(flat[:, OUT:OUT + HD], probT[:, i % 2, P * b:P * (b + 1)],
                                                 va[:, kt, HD * head:HD * (head + 1)], start=(b == 0),
                                                 stop=(b == 3 * blocks - 1), skip_group_check=True)
                    elif kind == "B":
                        for a, hd in enumerate(heads):
                            kv = hd // 4
                            for br in (0, 1):
                                r = 2 * a + br
                                for kt in range(blocks):
                                    b = r * blocks + kt
                                    last = pe.matmul(flat[:, OUT + HD * r:OUT + HD * (r + 1)], probT[:, i % 2, P * b:P * (b + 1)],
                                                     bv[:, kt, br, HD * kv:HD * (kv + 1)], start=(kt == 0),
                                                     stop=(kt == blocks - 1), skip_group_check=True)
                    else:
                        last = pe.matmul(ps[:, 7, :], probT[:, i % 2, 0:P], vcbd[:, :, :].rearrange("p g d -> p (g d)"),
                                         start=True, stop=True)
                    last.then_inc(pv_done, 1)

                scores(0)
                for i in range(NI):
                    if i + 1 < NI:
                        scores(i + 1)
                    else:
                        branch(("wa",), 0, 2, 0, 0, (1,)).then_inc(wa_done, 1)
                    if i:
                        values(i - 1)
                    filler(i)
                    prob_turn(i)
                branch(("wa",), 0, 2, 512, 2, (0,), (0,))
                values(NI - 1)
                branch(("wa",), 0, 2, 512, 2, (0,), (1,))

                pe.wait_ge(o_evac, NI * (layer + 1))
                for g in (1, 2):
                    outputs_turn_y(g)
                branch(("wa",), 0, 2, 512, 2, (1,)).then_inc(unit_used, 1)
                pe.wait_ge(yT_lo_ready, layer * PER["yt"] + 3)
                branch(("wb", 0), 2, 4, 0, 4).then_inc(unit_used, 1)
                branch(("wb", 1), 2, 4, 0, 6, range(3))

                def merged_turn(n):
                    pe.wait_ge(merged, 2 * layer + n + 1)
                    for tt in range(TT):
                        turn(hT_turned, 4 * n + tt, [gates[:, n, tt, P * b:P * (b + 1)] for b in range(4)])

                def mix(n, half, tt, tiles=range(4)):
                    whi, wlo = take(layer, ("mix", n, half))
                    cols = slice(tt * P, (tt + 1) * P)
                    for kk in tiles:
                        k = 4 * half + kk
                        last = product(ps[:, 2 * tt + n, :], hT_hi[:, k, cols], hT_lo[:, k, cols],
                                       whi[:, kk, :], wlo[:, kk, :], k == 0, k == 7)
                    return last

                merged_turn(0)
                branch(("wb", 1), 2, 4, 0, 6, range(3, 4)).then_inc(unit_used, 1)
                pe.wait_ge(hT_lo_ready, ht + 2)
                mix(0, 0, 0)
                mix(1, 0, 0)
                merged_turn(1)
                mix(0, 0, 1).then_inc(unit_used, 1)
                pe.wait_ge(hT_lo_ready, ht + 4)
                mix(0, 1, 0)
                mix(1, 1, 0).then_inc(res_done, 1)
                mix(1, 0, 1).then_inc(unit_used, 1)
                mix(0, 1, 1).then_inc(unit_used, 1)
                mix(1, 1, 1, range(2))
                layer_norm_turn(layer, 0, 0)
                mix(1, 1, 1, range(2, 4)).then_inc(unit_used, 1)

                xn = layer * PER["x"]

                def queries(tt):
                    pe.wait_ge(hT_lo_ready, ht + 6 + 2 * tt)
                    whi, wlo = take(layer, ("xq",))
                    cols = slice(tt * P, (tt + 1) * P)
                    for k in range(KT):
                        last = product(ps[:, 4 + 2 * tt, 0:S], hT_hi[:, k, cols], hT_lo[:, k, cols],
                                       whi[:, k, :], wlo[:, k, :], k == 0, k == KT - 1)
                    last.then_inc(xq_done if tt == 0 else unit_used, 1)

                def queries_turn(tt):
                    pe.wait_ge(xqn_ready, layer * TT + tt + 1)
                    turn(xqT_done, 5 + 2 * tt, [xq_n[:, tt, P * j:P * (j + 1)] for j in (0, 1)])

                def x_score(x):
                    tt, j = x // 2, x % 2
                    pe.wait_ge(xq_ready, layer * TT + tt + 1)
                    if x >= 2:
                        pe.wait_ge(x_exp, xn + x - 1)
                    for p in (0, 1):
                        part = slice(HD * p, HD * (p + 1))
                        last = pe.matmul(ps[:, 2 * (x % 2) + p, 0:S], xqT[part, j, tt * P:(tt + 1) * P],
                                         xkT[part, j, :], start=True, stop=True, skip_group_check=True)
                    last.then_inc(x_scores, 1)

                def x_turn(x):
                    pe.wait_ge(x_exp, xn + x + 1)
                    if x >= 2:
                        pe.wait_ge(x_probT, xn + x - 1)
                    turn(x_turned, 4 + x % 2, [xprob[:, x % 2, P * b:P * (b + 1)] for b in range(4)])

                def x_values(x):
                    j = x % 2
                    pe.wait_ge(x_probT, xn + x + 1)
                    if x >= 2:
                        pe.wait_ge(x_evac, xn + x - 1)
                    for p in (0, 1):
                        for kt in (0, 1):
                            b = 2 * p + kt
                            last = pe.matmul(ps[:, 6 + x % 2, HD * p:HD * (p + 1)], probT[:, x % 2, P * b:P * (b + 1)],
                                             xv[:, kt, HD * (2 * j + p):HD * (2 * j + p + 1)], start=(kt == 0),
                                             stop=(kt == 1), skip_group_check=True)
                    last.then_inc(x_pv, 1)

                def outputs_turn(tt):
                    pe.wait_ge(x_evac, xn + 2 * tt + 2)
                    turn(xoT_done, 4 * tt, [xo_n[:, tt, P * t:P * (t + 1)] for t in (0, 1)])

                def output_product(tt):
                    pe.wait_ge(xoT_lo_ready, layer * TT + tt + 1)
                    whi, wlo = take(layer, ("xo",))
                    cols = slice(tt * P, (tt + 1) * P)
                    for n in (0, 1):
                        for k in (0, 1):
                            last = product(ps[:, 2 * tt + n, :], xoT_hi[:, k, cols], xoT_lo[:, k, cols],
                                           whi[:, k, 512 * n:512 * (n + 1)], wlo[:, k, 512 * n:512 * (n + 1)], k == 0, k == 1)
                    last.then_inc(res_done if tt == 0 else unit_used, 1)

                if layer == 0:
                    memory_product(0, 0, range(4), 0).then_inc(unit_used, 1)
                    queries(0)
                    memory_product(0, 1, range(2), 0)
                    queries_turn(0)
                    layer_norm_turn(layer, 0, 1)
                    memory_product(0, 1, range(2, 4), 0).then_inc(unit_used, 1)
                    pe.wait_ge(xkv_ready, 1)
                    x_score(0)
                    queries(1)
                    x_turn(0)
                    x_score(1)
                else:
                    queries(0)
                    queries_turn(0)
                    x_score(0)
                    keep_warm(7, 14)
                    layer_norm_turn(layer, 0, 1)
                    x_score(1)
                    x_turn(0)
                    queries(1)
                queries_turn(1)
                x_score(2)
                x_turn(1)
                x_values(0)
                pe.wait_ge(xq_ready, (layer + 1) * TT)
                x_score(3)
                x_values(1)
                x_turn(2)
                x_turn(3)
                x_values(2)
                outputs_turn(0)
                x_values(3)
                outputs_turn(1)
                output_product(0)
                output_product(1)
                for tt in range(TT):
                    if layer < DEPTH - 1:
                        memory_product(layer + 1, tt, range(4), 6).then_inc(unit_used, 1)
                    else:
                        keep_warm(6, (16, 22)[tt])
                    layer_norm_turn(layer, 1, tt)

                pe.wait_ge(hT_lo_ready, ht + 12)

                def down(it):
                    pe.wait_ge(hid_lo_ready, layer * PER["ffn"] + it + 1)
                    whi, wlo = take(layer, ("down", it))
                    for tt in range(TT):
                        cols = slice(tt * P, (tt + 1) * P)
                        for n in (0, 1):
                            for k in (0, 1):
                                last = product(ps[:, 2 * tt + n, :], hid_hi[:, it % 2, k, cols], hid_lo[:, it % 2, k, cols],
                                               whi[:, k, 512 * n:512 * (n + 1)], wlo[:, k, 512 * n:512 * (n + 1)],
                                               it == 0 and k == 0, it == FF_IT - 1 and k == 1)
                        if tt == 1:
                            last.then_inc(unit_used, 1)
                        elif it == FF_IT - 1:
                            last.then_inc(res_done, 1)

                for it in range(FF_IT):
                    if it == 1 and layer < DEPTH - 1:
                        pe.wait_ge(xkv_ready, layer + 2)
                    for ag, name in enumerate(("ua", "ug")):
                        if it >= 2:
                            pe.wait_ge(conv_done, layer * PER["conv"] + 2 * (it - 2) + ag + 1)
                        whi, wlo = take(layer, (name, it))
                        for j in (0, 1):
                            cols = slice(j * P, (j + 1) * P)
                            for k in range(KT):
                                last = product(ps[:, 4 + 2 * (it % 2) + ag, S * j:S * (j + 1)], whi[:, k, cols], wlo[:, k, cols],
                                               hT_hi[:, k, :], hT_lo[:, k, :], k == 0, k == KT - 1)
                        last.then_inc(unit_used, 1)
                    if it:
                        down(it - 1)
                down(FF_IT - 1)
                if layer < DEPTH - 1:
                    pe.wait_ge(conv_done, PER["conv"] * (layer + 1))
                    keep_warm(6, 16)


_INS = ["x", "mem", "w_in", "cmp_pos", "cmp_w1", "cmp_b1", "cmp_w2", "w_branch_a", "w_branch_b", "w_mix_out",
        "ln1_g", "ln1_b", "w_xq", "w_xkv", "w_xo", "ln2_g", "ln2_b", "w_up", "conv_w", "conv_b", "w_down",
        "ln3_g", "ln3_b"]


def kernel(**inputs):
    import concourse.bacc as bacc
    from concourse.bass_utils import run_bass_kernel_spmd

    nc = bacc.Bacc("TRN2", target_bir_lowering=False, num_devices=1)
    arrays = {f"in_{name}": np.ascontiguousarray(inputs[name]) for name in _INS}
    arrays["const_f"], arrays["const_b"] = shape_constants()
    aps = {name: nc.dram_tensor(name, list(a.shape), mybir.dt.from_np(a.dtype), kind="ExternalInput").ap()
           for name, a in arrays.items()}
    out = nc.dram_tensor("out", [1, S, D], F32, kind="ExternalOutput").ap()
    hybrid_decoder_kernel(nc, {name: aps[f"in_{name}"] for name in _INS}, aps["const_f"], aps["const_b"], out)
    result = run_bass_kernel_spmd(nc, [arrays], core_ids=[0])
    return result.results[0]["out"]
```
